# Optimizing a Trainium2 kernel written in Bass

```python
import jax, jax.numpy as jnp
from jax import lax
import numpy as np

D_MODEL = 1024
BATCH = 1
SEQ = 512
DEPTH = 1

CHUNK = 64
HEAD_DIM = 64
ROPE_THETA = 10000.0
EPS = 1e-6
MAX_POS_OFFSET = 4096

SWA_Q_HEADS = 8
SWA_KV_HEADS = 2
SWA_WINDOW = 128
SWA_WINDOW_CHUNKS = SWA_WINDOW // CHUNK
SWA_Q_W = SWA_Q_HEADS * HEAD_DIM
SWA_KV_W = SWA_KV_HEADS * HEAD_DIM

SB_HEADS = 8
SB_W = SB_HEADS * HEAD_DIM
SB_QBLOCK = 128

IN_SPLITS = (SWA_Q_W, SWA_KV_W, SWA_KV_W, SB_W, SB_W, SB_W, D_MODEL, D_MODEL)
IN_W = sum(IN_SPLITS)

PEER_HEADS = 8
PEER_NKEYS = 128
PEER_EXPERTS = PEER_NKEYS * PEER_NKEYS
PEER_TOPK = 16
PEER_DKEY = 256
PEER_HALF = PEER_DKEY // 2
PEER_TOKEN_BLOCK = 128

N_MOD = 6

kernel_name = 'hybrid_swa_stickbreak_peer_block'

def rmsnorm(x, g):
    xf = x.astype(jnp.float32)
    y = xf * lax.rsqrt(jnp.mean(xf * xf, axis=-1, keepdims=True) + EPS)
    return (y * g.astype(jnp.float32)).astype(x.dtype)

def modulate(h, shift, scale):
    return h * (1 + scale[:, None, :]) + shift[:, None, :]

def rope(t, positions):
    half = HEAD_DIM // 2
    inv = ROPE_THETA ** (-jnp.arange(half, dtype=jnp.float32) / half)
    ang = positions.astype(jnp.float32)[..., None] * inv
    cos = jnp.cos(ang)[:, :, None, :].astype(t.dtype)
    sin = jnp.sin(ang)[:, :, None, :].astype(t.dtype)
    t1, t2 = t[..., :half], t[..., half:]
    return jnp.concatenate([t1 * cos - t2 * sin, t2 * cos + t1 * sin], axis=-1)

def swa_sink_attention(q, k, v, sinks):
    B, S = q.shape[0], q.shape[1]
    nc = S // CHUNK
    G = SWA_KV_HEADS
    R = SWA_Q_HEADS // G
    qc = q.reshape(B, nc, CHUNK, G, R, HEAD_DIM)
    kc = k.reshape(B, nc, CHUNK, G, HEAD_DIM)
    vc = v.reshape(B, nc, CHUNK, G, HEAD_DIM)

    def band(t):
        parts = []
        for w in range(SWA_WINDOW_CHUNKS - 1, -1, -1):
            pad = ((0, 0), (w, 0)) + ((0, 0),) * (t.ndim - 2)
            parts.append(jnp.pad(t, pad)[:, :nc])
        return jnp.concatenate(parts, axis=2)

    kw, vw = band(kc), band(vc)
    nk = SWA_WINDOW_CHUNKS * CHUNK
    key_chunk = (jnp.arange(nc)[:, None] - (SWA_WINDOW_CHUNKS - 1)
                 + jnp.arange(nk)[None, :] // CHUNK)
    valid = (key_chunk >= 0)[None, :, None, None, None, :]
    s = jnp.einsum('bncgrd,bnkgd->bngrck', qc, kw).astype(jnp.float32) * (HEAD_DIM ** -0.5)
    s = jnp.where(valid, s, -jnp.inf)
    sink = sinks.astype(jnp.float32).reshape(1, 1, G, R, 1, 1)
    m = jnp.maximum(jnp.max(s, axis=-1, keepdims=True), sink)
    e = jnp.exp(s - m)
    p = (e / (jnp.sum(e, axis=-1, keepdims=True) + jnp.exp(sink - m))).astype(v.dtype)
    o = jnp.einsum('bngrck,bnkgd->bncgrd', p, vw)
    return o.reshape(B, S, SWA_Q_W)

def stick_breaking_attention(q, k, v):
    B, S, H = q.shape[0], q.shape[1], q.shape[2]
    nb = S // SB_QBLOCK
    qh = q.transpose(0, 2, 1, 3)
    kh = k.transpose(0, 2, 1, 3)
    vh = v.transpose(0, 2, 1, 3)
    qblocks = qh.reshape(B, H, nb, SB_QBLOCK, HEAD_DIM).transpose(2, 0, 1, 3, 4)
    key_pos = jnp.arange(S)

    def block(args):
        qb, bi = args
        z = jnp.einsum('bhqd,bhkd->bhqk', qb, kh).astype(jnp.float32) * (HEAD_DIM ** -0.5)
        q_pos = bi * SB_QBLOCK + jnp.arange(SB_QBLOCK)
        causal = key_pos[None, :] < q_pos[:, None]
        log_1mb = jnp.where(causal, jax.nn.log_sigmoid(-z), 0.0)
        after = lax.cumsum(log_1mb, axis=3, reverse=True) - log_1mb
        log_a = jnp.where(causal, jax.nn.log_sigmoid(z) + after, -jnp.inf)
        a = jnp.exp(log_a).astype(vh.dtype)
        return jnp.einsum('bhqk,bhkd->bhqd', a, vh)

    o = lax.map(block, (qblocks, jnp.arange(nb)))
    return o.transpose(1, 0, 3, 2, 4).reshape(B, S, SB_W)

def peer(h, w_query, sub_keys, expert_u, expert_v):
    B, S, D = h.shape
    K = PEER_TOPK
    qry = (h @ w_query).reshape(B, S, PEER_HEADS, 2, PEER_HALF)
    sc = jnp.einsum('bshpd,hpnd->bshpn', qry, sub_keys)
    top_s, top_i = lax.top_k(sc, K)
    cand = top_s[..., 0, :, None] + top_s[..., 1, None, :]
    best, flat = lax.top_k(cand.reshape(B, S, PEER_HEADS, K * K), K)
    i1 = flat // K
    i2 = flat % K
    experts = (jnp.take_along_axis(top_i[..., 0, :], i1, axis=-1) * PEER_NKEYS
               + jnp.take_along_axis(top_i[..., 1, :], i2, axis=-1))
    g = jax.nn.softmax(best.astype(jnp.float32), axis=-1).astype(h.dtype)
    nblk = (B * S) // PEER_TOKEN_BLOCK
    hb = h.reshape(nblk, PEER_TOKEN_BLOCK, D)
    eb = experts.reshape(nblk, PEER_TOKEN_BLOCK, PEER_HEADS * K)
    gb = g.reshape(nblk, PEER_TOKEN_BLOCK, PEER_HEADS * K)

    def block(args):
        xt, et, gt = args
        u = expert_u[et]
        act = jax.nn.gelu(jnp.einsum('td,tkd->tk', xt, u), approximate=False) * gt
        return jnp.einsum('tk,tkd->td', act, expert_v[et])

    return lax.map(block, (hb, eb, gb)).reshape(B, S, D)

def setup_inputs(seed: int = 0) -> dict:
    key = jax.random.key(seed)
    ks = jax.random.split(key, 18)
    f32 = jnp.float32
    D = D_MODEL
    x = jax.random.normal(ks[0], (BATCH, SEQ, D), f32)
    c = jax.random.normal(ks[1], (BATCH, D), f32)
    offs = jax.random.randint(ks[2], (BATCH, 1), 0, MAX_POS_OFFSET, dtype=jnp.int32)
    positions = offs + jnp.arange(SEQ, dtype=jnp.int32)[None, :]
    norm1_g = 1.0 + 0.02 * jax.random.normal(ks[3], (DEPTH, D), f32)
    norm2_g = 1.0 + 0.02 * jax.random.normal(ks[4], (DEPTH, D), f32)
    final_g = 1.0 + 0.02 * jax.random.normal(ks[5], (D,), f32)
    w_ada = jax.random.normal(ks[6], (DEPTH, D, N_MOD * D), f32) * D ** -0.5
    b_ada = 0.02 * jax.random.normal(ks[7], (DEPTH, N_MOD * D), f32)
    w_in = jax.random.normal(ks[8], (DEPTH, D, IN_W), f32) * D ** -0.5
    sinks = 0.5 * jax.random.normal(ks[9], (DEPTH, SWA_Q_HEADS), f32)
    w_up_swa = jax.random.normal(ks[10], (DEPTH, SWA_Q_W, D), f32) * SWA_Q_W ** -0.5
    w_up_sb = jax.random.normal(ks[11], (DEPTH, SB_W, D), f32) * SB_W ** -0.5
    w_out = jax.random.normal(ks[12], (DEPTH, D, D), f32) * D ** -0.5
    w_query = jax.random.normal(ks[13], (DEPTH, D, PEER_HEADS * PEER_DKEY), f32) * D ** -0.5
    sub_keys = jax.random.normal(ks[14], (DEPTH, PEER_HEADS, 2, PEER_NKEYS, PEER_HALF), f32) * PEER_HALF ** -0.5
    expert_u = jax.random.normal(ks[15], (DEPTH, PEER_EXPERTS, D), f32) * D ** -0.5
    expert_v = 0.5 * jax.random.normal(ks[16], (DEPTH, PEER_EXPERTS, D), f32)
    return {'x': x, 'c': c, 'positions': positions, 'norm1_g': norm1_g, 'norm2_g': norm2_g,
            'final_g': final_g, 'w_ada': w_ada, 'b_ada': b_ada, 'w_in': w_in, 'sinks': sinks,
            'w_up_swa': w_up_swa, 'w_up_sb': w_up_sb, 'w_out': w_out, 'w_query': w_query,
            'sub_keys': sub_keys, 'expert_u': expert_u, 'expert_v': expert_v}

def reference(x, c, positions, norm1_g, norm2_g, final_g, w_ada, b_ada, w_in, sinks,
              w_up_swa, w_up_sb, w_out, w_query, sub_keys, expert_u, expert_v):
    B, S, D = x.shape
    split_pts = list(np.cumsum(IN_SPLITS)[:-1])
    c_act = jax.nn.silu(c)
    for layer in range(DEPTH):
        mod = c_act @ w_ada[layer] + b_ada[layer]
        shift1, scale1, gate1, shift2, scale2, gate2 = jnp.split(mod, N_MOD, axis=-1)

        h = modulate(rmsnorm(x, norm1_g[layer]), shift1, scale1)
        proj = h @ w_in[layer]
        qa, ka, va, qb, kb, vb, ga, gb = jnp.split(proj, split_pts, axis=-1)
        qa = rope(qa.reshape(B, S, SWA_Q_HEADS, HEAD_DIM), positions)
        ka = rope(ka.reshape(B, S, SWA_KV_HEADS, HEAD_DIM), positions)
        va = va.reshape(B, S, SWA_KV_HEADS, HEAD_DIM)
        ya = swa_sink_attention(qa, ka, va, sinks[layer]) @ w_up_swa[layer]
        yb = stick_breaking_attention(qb.reshape(B, S, SB_HEADS, HEAD_DIM),
                                      kb.reshape(B, S, SB_HEADS, HEAD_DIM),
                                      vb.reshape(B, S, SB_HEADS, HEAD_DIM)) @ w_up_sb[layer]
        merged = jax.nn.sigmoid(ga) * ya + jax.nn.sigmoid(gb) * yb
        x = x + gate1[:, None, :] * (merged @ w_out[layer])

        h2 = modulate(rmsnorm(x, norm2_g[layer]), shift2, scale2)
        x = x + gate2[:, None, :] * peer(h2, w_query[layer], sub_keys[layer],
                                          expert_u[layer], expert_v[layer])
    return rmsnorm(x, final_g)


_drawn_inputs = setup_inputs


def setup_inputs(seed=0):
    import zlib

    import numpy as np

    out = dict(_drawn_inputs(seed))
    spreads = {}
    factors = {'norm1_g': 3.198, 'final_g': 2.694, 'sinks': 64.0, 'norm2_g': 4.296}
    for name, (base, spread) in spreads.items():
        noise = np.random.default_rng([zlib.crc32(name.encode()), seed]).standard_normal(out[name].shape)
        drawn = base * np.exp(spread * noise) if base else spread * noise
        out[name] = __import__('jax').numpy.asarray(drawn.astype(out[name].dtype))
    for name, factor in factors.items():
        out[name] = (out[name] * factor).astype(out[name].dtype)
    return out
```

```python
from contextlib import ExitStack

import numpy as np
import concourse.bass as bass
from concourse import mybir

P = 128
T = 512
D = 1024
TT = T // P
DC = D // P
NMOD = 6
HD = 64
PAIRS = 4
HEADS = 8
TOPK = 16
NK = 128
EG = 4
ADA = (5, 5, 1, 1)
FREE = 1
EPS = 1e-6
BIG = -1e30
LOWEST = -3.0e38
MAGIC = 12582912.0
TWO_PI = 2 * np.pi
C1 = 6.28125
C2 = float(np.float32(1935.0 * 2.0 ** -20))
C3 = float(TWO_PI - C1 - C2)

ALU = mybir.AluOpType
ACT = mybir.ActivationFunctionType
F32 = mybir.dt.float32
F32R = mybir.dt.float32r
U32 = mybir.dt.uint32
I32 = mybir.dt.int32
AX = mybir.AxisListType

(K_ID, K_ONE, K_NTRI, K_NONE, K_SBM, K_CAUS, K_ROT, K_IOTA, K_SWA0, K_SWA, K_INV, K_END) = (
    0, 128, 256, 384, 512, 640, 768, 896, 1024, 1280, 1536, 1537)
S_C, S_G1, S_G2, S_GF, S_B, S_SINK, S_END = 0, 8, 16, 24, 32, 80, 88


class Steps:

    def __init__(self, engine, sem):
        self.engine, self.sem, self.n, self.at = engine, sem, 0, 0

    def __call__(self, instruction, apart=False):
        instruction.then_inc(self.sem, 1)
        self.n += 1
        if apart:
            self.wait_apart(self.sem, self.at + self.n)
        else:
            self.engine.wait_ge(self.sem, self.at + self.n)

    def wait_apart(self, sem, value):
        self.engine.wait_ge(sem, value)
        self.engine.memset(self.pad, 0.0)

    def enter(self, i, per_turn):
        self.before, self.per = self.n, per_turn
        self.at, self.n = i * per_turn + self.before, 0

    def leave(self, turns):
        assert self.n == self.per, (self.n, self.per)
        self.at, self.n = 0, self.before + turns * self.per


def row(a, i):
    return a[bass.ds(i, 1), :, :].rearrange("a p n -> p (a n)")


def build(nc, xT, small, consts, pos, w_ada, w_kava, w_pair, w_gate, w_up, w_out, w_qry, skT, euT, ev, outT):
    with ExitStack() as ctx:
        def sb(name, shape, dt=F32):
            return ctx.enter_context(nc.sbuf_tensor(name, shape, dt))

        def sem(name):
            return ctx.enter_context(nc.semaphore(name))

        ps = [ctx.enter_context(nc.psum_tensor(f"bank{n}", [P, 512], F32)) for n in range(8)]
        gates_dram = nc.dram_tensor("gates_scratch", (NK, P, T), F32, kind="Internal").ap()

        cst = sb("cst", [P, K_END])
        sml = sb("sml", [P, S_END])
        x = sb("x", [P, DC, T])
        h = sb("h", [P, DC, T])
        mod = sb("mod", [P, NMOD * DC])
        mul1 = sb("mul1", [P, DC])
        mul2 = sb("mul2", [P, DC])
        cact = sb("cact", [P, DC])
        var = sb("var", [P, T])
        rstd = sb("rstd", [P, T])
        pad = sb("pad", [P, 1])
        ident = cst[:, K_ID:K_ID + P]
        ones = cst[:, K_ONE:K_ONE + P]

        def part(m, k=None):
            return mod[:, m * DC:(m + 1) * DC] if k is None else mod[:, m * DC + k:m * DC + k + 1]

        ARENA = 164 * 256
        arena_at = -(-nc.sbuf_base // 64) * 64
        arena = nc.alloc_sbuf_tensor_at("arena", [P, ARENA], F32, offset=arena_at)
        top = [0]

        def carve(*shape, split=None):
            n = int(np.prod(shape))
            if split:
                a = nc.alloc_sbuf_tensor_at(split, [P, n], F32R, offset=arena_at + 4 * top[0])[:]
            else:
                a = arena[:, top[0]:top[0] + n]
            top[0] += n
            assert top[0] <= ARENA, top[0]
            if len(shape) == 2:
                a = a.rearrange("p (a b) -> p a b", a=shape[0])
            if len(shape) == 3:
                a = a.rearrange("p (a b c) -> p a b c", a=shape[0], b=shape[1])
            return a

        ring = carve(4, 4096)
        front = top[0]
        pairw = carve(DC, 512)
        kavaw = pairw[:, :, 0:256]
        cosT = carve(T)
        sinT = carve(T)
        ang = carve(T)
        turn = carve(T)
        kR = carve(T)
        vA = carve(TT, P)
        qraw = carve(T)
        qR = carve(T)
        qB = carve(T)
        kB = carve(T)
        vB = carve(TT, P)
        prob = carve(TT, 256)
        probT = carve(TT, 256)
        spl = carve(4, T)
        atB = carve(4, T)
        adap = carve(2, T)
        mx = carve(8)
        sk4 = carve(16)
        att_end = top[0]
        top[0] = front
        siga = carve(2, T)
        sigb = carve(2, T)
        ma = carve(2, T)
        mb = carve(2, T)
        merged = carve(DC, T)
        yA = arena[:, ARENA - 2 * PAIRS * T:ARENA - PAIRS * T].rearrange("p (a b) -> p a b", a=PAIRS)
        yB = arena[:, ARENA - PAIRS * T:ARENA].rearrange("p (a b) -> p a b", a=PAIRS)
        assert max(top[0], att_end) <= ARENA - 2 * PAIRS * T, (top[0], att_end)
        squares2 = yB[:, 2:4, :]
        top[0] = 0
        stages = (carve(NK, 64), carve(NK, 64))
        ohi = carve(2, 4, P)
        ohj = carve(2, 4, P)
        slotsT = carve(3, T)
        top_k_at = top[0]
        skt = carve(2 * HEADS, P)
        qv = carve(2, T)
        sc = carve(2, TT, P)
        sc2 = carve(2, TT, P)
        tv = carve(2, TT, TOPK)
        ti = carve(2, TT, TOPK).bitcast(U32)
        tif = carve(2, TT, TOPK)
        cand = carve(TT, 256)
        cand2 = carve(TT, 256)
        bv = carve(TT, TOPK)
        bi = carve(TT, TOPK).bitcast(U32)
        bij = carve(2, TT * TOPK).bitcast(U32)
        bijf = carve(2, TT * TOPK)
        pick = carve(2, TT * TOPK, TOPK)
        den = carve(2 * TT)
        slots = carve(3, TT, P)
        top_k_end = top[0]
        top[0] = 0
        vs = carve(2, EG * D, split="v_split")
        ar = carve(EG, 2, T, split="a_split")
        vt = carve(EG * D)
        gel = carve(EG, T)
        wg_ = carve(2, T)
        gt = carve(2, T)
        top[0] = max(top[0], top_k_at)
        ut = carve(EG, DC * P)
        us = carve(EG, 2, DC * P, split="u_split")
        hs_at = top[0]
        assert hs_at >= top_k_end, (hs_at, top_k_end)
        hs = carve(2 * DC, T, split="h_split").rearrange("p (s k) n -> p s k n", s=2)
        acc = h[:]

        smalls_in, x_in, kava_in, pair_in, sk_in = map(sem, ("smalls_in", "x_in", "kava_in", "pair_in", "sk_in"))
        ring_in = [sem(f"ring_in{s}") for s in range(4)]
        ring_free = [sem(f"ring_free{s}") for s in range(4)]
        ada_ready, ada_summed = sem("ada_ready"), sem("ada_summed")
        hi_ready, h_split, u_hi, u_split, v_hi, v_split, a_split = map(sem, (
            "hi_ready", "h_split", "u_hi", "u_split", "v_hi", "v_split", "a_split"))
        cact_ready, mod_ready = sem("cact_ready"), sem("mod_ready")
        sq_ready, sq_summed, var_ready, root_ready, norm_part, h_ready = map(sem, (
            "sq_ready", "sq_summed", "var_ready", "root_ready", "norm_part", "h_ready"))
        dve_steps, act_steps = sem("dve_steps"), sem("act_steps")
        angle_ready, trig_ready = sem("angle_ready"), sem("trig_ready")
        proj_done, q_raw_ready, rot_done, rope_ready, evac_done = map(sem, (
            "proj_done", "q_raw_ready", "rot_done", "rope_ready", "evac_done"))
        va_done, va_ready = sem("va_done"), sem("va_ready")
        swa_scored, max_ready, swa_exp, prob_ready, probT_done, probT_ready, oa_done, oa_out = map(sem, (
            "swa_scored", "max_ready", "swa_exp", "prob_ready", "probT_done", "probT_ready", "oa_done", "oa_out"))
        sb_scored, abs_ready, log_ready, sp_ready, sb_summed, at_ready, ob_done, ob_out = map(sem, (
            "sb_scored", "abs_ready", "log_ready", "sp_ready", "sb_summed", "at_ready", "ob_done", "ob_out"))
        gate_done, sig_ready, up_done, merged_ready = map(sem, ("gate_done", "sig_ready", "up_done", "merged_ready"))
        out_done, x_ready = sem("out_done"), sem("x_ready")
        qry_done, qry_ready, score_done, score_ready, score_used = map(sem, (
            "qry_done", "qry_ready", "score_done", "score_ready", "score_used"))
        best_ready, best_exp, slots_ready, slotsT_done, slotsT_ready = map(sem, (
            "best_ready", "best_exp", "slots_ready", "slotsT_done", "slotsT_ready"))
        hot_ready = [sem("hot_ready0"), sem("hot_ready1")]
        hot_done = [sem("hot_done0"), sem("hot_done1")]
        staged = [sem("staged0"), sem("staged1")]
        g_out = [sem("g_out0"), sem("g_out1")]
        u_in = [sem(f"u_in{e}") for e in range(EG)]
        g_in = [sem(f"g_in{e}") for e in range(2)]
        v_in = [sem(f"v_in{e}") for e in range(EG)]
        s_done, gelu_ready, w_ready, a_hi, v_done, acc_zero, acc_ready = map(sem, (
            "s_done", "gelu_ready", "w_ready", "a_hi", "v_done", "acc_zero", "acc_ready"))
        y_ready, y_out = sem("y_ready"), sem("y_out")
        GROUPS = NK // EG

        def start(engine, *sems):
            for s in sems:
                engine.sem_inc(s, FREE)

        block = ctx.enter_context(nc.Block())

        @block.sync
        def _(sp):
            start(sp, *g_out)
            sp.dma_start(sml[:], small).then_inc(smalls_in, 16)
            sp.dma_start(cst[:], consts).then_inc(smalls_in, 16)
            sp.dma_start(ang.bitcast(I32), pos.to_broadcast([P, T])).then_inc(smalls_in, 16)
            sp.dma_start(x[:], xT).then_inc(x_in, 16)
            for n in range(4):
                sp.dma_start(ring[:, n, :], w_ada[n]).then_inc(ring_in[n], 16)
            sp.dma_start(kavaw, w_kava).then_inc(kava_in, 16)
            with sp.Fori(0, PAIRS) as i:
                for a in range(2):
                    sp.wait_ge(ring_free[a], i + 1 + FREE)
                    sp.dma_start(ring[:, a, :], row(w_ada, i * 2 + (4 + a))).then_inc(ring_in[a], 16)
            for m in range(DC):
                s = m % 4
                if m < 4:
                    sp.wait_ge(ring_free[s], ADA[s] + FREE)
                else:
                    sp.wait_ge(up_done, s + 1)
                sp.dma_start(ring[:, s, 0:2048], w_gate[m]).then_inc(ring_in[s], 16)
                sp.dma_start(ring[:, s, 2048:3072], w_up[m]).then_inc(ring_in[s], 16)
            for s in range(2):
                sp.wait_ge(up_done, 4 + s + 1)
                sp.dma_start(ring[:, s, :].rearrange("p (m n) -> p m n", m=4),
                             w_out[4 * s:4 * s + 4, :, :].rearrange("m p n -> p m n")).then_inc(ring_in[s], 16)
            sp.wait_ge(out_done, DC)
            sp.dma_start(skt, skT).then_inc(sk_in, 16)
            with sp.Fori(0, HEADS // 2) as r:
                sp.wait_ge(qry_done, r * 4 + FREE)
                for s in range(2):
                    sp.dma_start(ring[:, 2 + s, 0:2048], row(w_qry, r * 2 + s)).then_inc(ring_in[2 + s], 16)
            def load_u(g):
                for e in range(EG):
                    if isinstance(g, int) and g == 0:
                        sp.wait_ge(slotsT_ready, 3)
                    else:
                        sp.wait_ge(u_split, (g - 1) * EG + (e + 1))
                    sp.dma_start(ut[:, e, :], row(euT, g * EG + e)).then_inc(u_in[e], 16)

            def load_v(g):
                for e in range(EG):
                    if not isinstance(g, int) or g > 0:
                        sp.wait_ge(v_split, (g - 1) * EG + (e + 1))
                    sp.dma_start(vt[:, e * D:(e + 1) * D], row(ev, g * EG + e)).then_inc(v_in[e], 16)
                for e in range(EG):
                    if not isinstance(g, int) or g > 0 or e >= 2:
                        sp.wait_ge(w_ready, g * EG + (e - 1))
                    sp.dma_start(gt[:, e % 2, :], row(gates_dram, g * EG + e)).then_inc(g_in[e % 2], 16)

            load_u(0)
            with sp.Fori(0, T // 128) as q:
                for c in range(2):
                    for b in range(2):
                        sp.wait_ge(staged[b], q * 16 + (8 * c + 8) + FREE)
                    sp.dma_start(gates_dram[:, :, bass.ds(q * 128 + c * 64, 64)].rearrange("i j t -> j i t"),
                                 stages[c]).then_inc(g_out[c], 16)
            for c in range(2):
                sp.wait_ge(g_out[c], 16 * (T // 128) + FREE)

            load_u(1)
            load_v(0)
            load_u(2)
            with sp.Fori(2, GROUPS - 1) as g:
                load_v(g - 1)
                load_u(g + 1)
            load_v(GROUPS - 2)
            load_v(GROUPS - 1)
            sp.wait_ge(y_ready, DC)
            sp.dma_start(outT, h[:]).then_inc(y_out, 16)
            sp.wait_ge(y_out, 16)

        @block.gpsimd
        def _(pool):
            pool.wait_ge(va_done, 1)
            with pool.Fori(0, PAIRS) as i:
                pool.wait_ge(proj_done, i * 4 + 1)
                pool.dma_start(pairw.rearrange("p k n -> p (k n)"), row(w_pair, i)).then_inc(pair_in, 16)

        @block.tensor
        def _(pe):
            start(pe, *hot_done, qry_done, score_done, v_done)
            def rms_sum(first, squares):
                for k in range(DC):
                    pe.wait_ge(sq_ready, first + k + 1)
                    pe.matmul(ps[7][:], ones, squares[:, k % 2, :], start=(k == 0), stop=(k == DC - 1)).then_inc(sq_summed, 1)

            def ada_sum(n, b, bank, col):
                pe.wait_ge(ada_ready, n + 1)
                for m in range(4):
                    last = pe.matmul(bank[:, bass.ds(col + m, 1)], adap[:, b, m * P:(m + 1) * P], ones[:, 0:1], start=True, stop=True)
                last.then_inc(ada_summed, 1)

            rms_sum(0, spl)
            for n in range(4):
                ada_sum(n, n % 2, ps[6], n * 4)
            pe.wait_ge(h_ready, DC)
            pe.wait_ge(kava_in, 16)
            for k in range(DC):
                last = pe.matmul(ps[0][:], kavaw[:, k, 0:P], h[:, k, :], start=(k == 0), stop=(k == DC - 1))
            last.then_inc(proj_done, 1)
            for t in range(TT):
                for k in range(DC):
                    last = pe.matmul(ps[1][:, t * P:(t + 1) * P], h[:, k, t * P:(t + 1) * P], kavaw[:, k, P:2 * P],
                                     start=(k == 0), stop=(k == DC - 1))
            last.then_inc(va_done, 1)
            pe.wait_ge(q_raw_ready, 1)
            pe.matmul(ps[4][:], cst[:, K_ROT:K_ROT + P], qraw, start=True, stop=True).then_inc(rot_done, 1)
            pe.wait_ge(va_ready, 1)
            pe.wait_ge(rope_ready, 1)

            with pe.Fori(0, PAIRS) as i:
                pe.wait_ge(pair_in, i * 16 + 16)
                pe.wait_ge(oa_out, i * 2 + FREE)
                pe.wait_ge(ob_out, i * 2 + FREE)
                for c in range(3):
                    for k in range(DC):
                        last = pe.matmul(ps[c][:], pairw[:, k, c * P:(c + 1) * P], h[:, k, :], start=(k == 0), stop=(k == DC - 1))
                    last.then_inc(proj_done, 1)
                for t in range(TT):
                    for k in range(DC):
                        last = pe.matmul(ps[3][:, t * P:(t + 1) * P], h[:, k, t * P:(t + 1) * P], pairw[:, k, 3 * P:4 * P],
                                         start=(k == 0), stop=(k == DC - 1))
                last.then_inc(proj_done, 1)
                for a in range(2):
                    ada_sum(i * 2 + (4 + a), a, ps[7], i * 8 + 4 * a)
                pe.wait_ge(q_raw_ready, i + 2)
                pe.wait_ge(at_ready, i * 8 + FREE)
                pe.matmul(ps[4][:], cst[:, K_ROT:K_ROT + P], qraw, start=True, stop=True).then_inc(rot_done, 1)
                pe.wait_ge(evac_done, i * 3 + 3)
                pe.wait_ge(rope_ready, i + 2)
                for a in range(2):
                    lo, hi = a * HD, (a + 1) * HD
                    for t in range(TT):
                        at = ps[t // 2][:, (t % 2) * 256:(t % 2) * 256 + 256]
                        mask = cst[:, K_SWA0:K_SWA0 + 256] if t == 0 else cst[:, K_SWA:K_SWA + 256]
                        pe.matmul(at, ident, mask, start=True, stop=False)
                        if t == 0:
                            last = pe.matmul(at[:, P:2 * P], qR[lo:hi, 0:P], kR[lo:hi, 0:P], start=False, stop=True)
                        else:
                            last = pe.matmul(at, qR[lo:hi, t * P:(t + 1) * P], kR[lo:hi, (t - 1) * P:(t + 1) * P],
                                             start=False, stop=True)
                    last.then_inc(swa_scored, 1)
                    pe.wait_ge(at_ready, i * 8 + a * 4 + FREE)
                    for b in range(4):
                        pe.matmul(ps[4 + b][:, b * P:T], kB[lo:hi, b * P:(b + 1) * P], qB[lo:hi, b * P:T],
                                  start=True, stop=True).then_inc(sb_scored, 1)
                    pe.wait_ge(prob_ready, i * 2 + (a + 1))
                    for t in range(TT):
                        for c in range(2):
                            last = pe.transpose(ps[2 + t // 2][:, (t % 2) * 256 + c * P:(t % 2) * 256 + (c + 1) * P],
                                                prob[:, t, c * P:(c + 1) * P], ident)
                    last.then_inc(probT_done, 1)
                    pe.wait_ge(sp_ready, i * 8 + (a * 4 + 4))
                    for b in range(4):
                        pe.matmul(ps[4 + b][:, b * P:T], cst[:, K_NTRI:K_NTRI + P], spl[:, b, b * P:T], start=False, stop=False,
                                  skip_group_check=True)
                        for c in range(b + 1, 4):
                            pe.matmul(ps[4 + b][:, c * P:T], cst[:, K_NONE:K_NONE + P], spl[:, c, c * P:T], start=False, stop=False,
                                      skip_group_check=True)
                        pe.matmul(ps[4 + b][:, b * P:(b + 1) * P], ident, cst[:, K_SBM:K_SBM + P], start=False, stop=True,
                                  skip_group_check=True).then_inc(sb_summed, 1)
                    pe.wait_ge(probT_ready, i * 2 + (a + 1))
                    for t in range(TT):
                        for c in ((1,) if t == 0 else (0, 1)):
                            last = pe.matmul(ps[0][lo:hi, t * P:(t + 1) * P], vA[:, t - 1 + c, lo:hi],
                                             probT[:, t, c * P:(c + 1) * P], start=(c == 0 or t == 0), stop=(c == 1))
                    last.then_inc(oa_done, 1)
                    for b in range(4):
                        pe.wait_ge(at_ready, i * 8 + (a * 4 + b + 1) + FREE)
                        last = pe.matmul(ps[1][lo:hi, b * P:T], vB[:, b, lo:hi], atB[:, b, b * P:T], start=(b == 0), stop=(b == 3),
                                         skip_group_check=True)
                    last.then_inc(ob_done, 1)
                    if a == 0:
                        pe.wait_ge(oa_out, i * 2 + 1 + FREE)
                        pe.wait_ge(ob_out, i * 2 + 1 + FREE)

            pe.wait_ge(oa_out, 2 * PAIRS + FREE)
            pe.wait_ge(ob_out, 2 * PAIRS + FREE)
            pe.wait_ge(mod_ready, 2)
            with pe.Fori(0, 2) as r:
                for s in range(4):
                    b = 4 * (s % 2)
                    pe.wait_ge(ring_in[s], r * 32 + (16 * ADA[s] + 32))
                    pe.wait_ge(merged_ready, r * 4 + max(s - 1, 0) + FREE)
                    wg = ring[:, s, 0:2048].rearrange("p (k n) -> p k n", k=DC)
                    wu = ring[:, s, 2048:3072].rearrange("p (k n) -> p k n", k=2 * PAIRS)
                    for c in range(2):
                        for k in range(DC):
                            last = pe.matmul(ps[b + c][:], wg[:, k, c * P:(c + 1) * P], h[:, k, :], start=(k == 0), stop=(k == DC - 1))
                        last.then_inc(gate_done, 1)
                    for c, y in enumerate((yA, yB)):
                        for k in range(PAIRS):
                            last = pe.matmul(ps[b + 2 + c][:], wu[:, c * PAIRS + k, :], y[:, k, :], start=(k == 0), stop=(k == PAIRS - 1))
                    last.then_inc(up_done, 1)
            pe.wait_ge(merged_ready, DC + FREE)
            for m in range(DC):
                if m % 4 == 0:
                    pe.wait_ge(ring_in[m // 4], 16 * ADA[m // 4] + 32 * 2 + 16)
                if m >= 2:
                    pe.wait_ge(x_ready, m - 1)
                w = ring[:, m // 4, (m % 4) * 1024:(m % 4 + 1) * 1024].rearrange("p (k n) -> p k n", k=DC)
                for k in range(DC):
                    last = pe.matmul(ps[m % 2][:], w[:, k, :], merged[:, k, :], start=(k == 0), stop=(k == DC - 1))
                last.then_inc(out_done, 1)
            rms_sum(DC, squares2)
            pe.wait_ge(h_ready, 2 * DC)
            pe.wait_ge(sk_in, 16)
            with pe.Fori(0, HEADS // 2) as r:
                for s in range(2):
                    pe.wait_ge(ring_in[2 + s], r * 16 + (16 * ADA[2 + s] + 32 * 2 + 16))
                    pe.wait_ge(qry_ready, r * 4 + s * 2 + FREE)
                    w = ring[:, 2 + s, 0:2048].rearrange("p (k n) -> p k n", k=DC)
                    for c in range(2):
                        for k in range(DC):
                            last = pe.matmul(ps[c][:], w[:, k, c * P:(c + 1) * P], h[:, k, :], start=(k == 0), stop=(k == DC - 1))
                        last.then_inc(qry_done, 1)
                    pe.wait_ge(qry_ready, r * 4 + (s * 2 + 2) + FREE)
                    pe.wait_ge(score_ready, r * 4 + s * 2 + FREE)
                    for c in range(2):
                        for t in range(TT):
                            last = pe.matmul(ps[2 + c][:, t * P:(t + 1) * P], qv[:, c, t * P:(t + 1) * P],
                                             skt[:, bass.ds(r * 4 + (s * 2 + c), 1), :].rearrange("p a n -> p (a n)"), start=True, stop=True)
                        last.then_inc(score_done, 1)
            pe.wait_ge(slots_ready, 3 * HEADS)
            pe.wait_ge(score_ready, 2 * HEADS + FREE)
            for f in range(3):
                for t in range(TT):
                    last = pe.transpose(ps[f][:, t * P:(t + 1) * P], slots[:, f, t, :], ident)
                last.then_inc(slotsT_done, 1)
            pe.wait_ge(slotsT_ready, 3)
            with pe.Fori(0, T // 8) as r:
                for b in range(2):
                    pe.wait_ge(hot_ready[b], r * 8 + 8)
                    pe.wait_ge(staged[b], r + FREE)
                    for q in range(4):
                        last = pe.matmul(ps[b][:, q * P:(q + 1) * P], ohj[:, b, q, :], ohi[:, b, q, :], start=True, stop=True)
                    last.then_inc(hot_done[b], 1)

            PASSES = ((0, 0), (1, 0), (0, 1))

            def scores(g):
                for e in range(EG):
                    pe.wait_ge(u_split, g * EG + (e + 1))
                    if isinstance(g, int) and g == 0 and e < 2:
                        pe.wait_ge(staged[e], T // 8 + FREE)
                    else:
                        pe.wait_ge(gelu_ready, g * EG + (e - 1))
                    for k in range(DC):
                        for q, (wp, xp) in enumerate(PASSES):
                            last = pe.matmul(ps[e % 2][:], us[:, e, wp, k * P:(k + 1) * P], hs[:, xp, k, :],
                                             start=(k == 0 and q == 0), stop=(k == DC - 1 and q == 2))
                    last.then_inc(s_done, 1)

            def values(g):
                pe.wait_ge(v_split, g * EG + EG)
                pe.wait_ge(a_split, g * EG + EG)
                for k in range(DC):
                    pe.wait_ge(acc_ready, g * DC + (max(k - 3, 0) + FREE))
                    for e in range(EG):
                        for q, (wp, xp) in enumerate(PASSES):
                            last = pe.matmul(ps[4 + k % 4][:], vs[:, wp, e * D + k * P:e * D + (k + 1) * P], ar[:, e, xp, :],
                                             start=(e == 0 and q == 0), stop=(e == EG - 1 and q == 2))
                    last.then_inc(v_done, 1)

            pe.wait_ge(h_split, DC)
            scores(0)
            scores(1)
            values(0)
            with pe.Fori(2, GROUPS) as g:
                scores(g)
                values(g - 1)
            values(GROUPS - 1)
            rms_sum(2 * DC, gel)

        @block.scalar
        def _(sa):
            start(sa, at_ready, qry_ready, score_ready, *staged)
            act_ = nc.scalar.activation

            def squares(first, dst):
                for k in range(DC):
                    if k >= 2:
                        sa.wait_ge(sq_summed, first + k - 1)
                    act_(dst[:, k % 2, :], x[:, k, :], ACT.Square).then_inc(sq_ready, 1)

            def root(n):
                sa.wait_ge(var_ready, n)
                act_(rstd[:], var[:], ACT.Sqrt).then_inc(root_ready, 1)

            def modulate(n, mul, shift):
                for k in range(DC):
                    sa.wait_ge(norm_part, n * DC + k + 1)
                    act_(h[:, k, :], h[:, k, :], ACT.Identity, scale=mul[:, k:k + 1], bias=part(shift, k)).then_inc(h_ready, 1)

            sa.wait_ge(smalls_in, 48)
            act_(cact[:], sml[:, S_C:S_C + DC], ACT.Silu).then_inc(cact_ready, 1)
            sa.wait_ge(angle_ready, 2)
            act_(sinT, sinT, ACT.Sin).then_inc(trig_ready, 1)
            act_(cosT, cosT, ACT.Sin).then_inc(trig_ready, 1)
            sa.wait_ge(x_in, 16)
            squares(0, spl)
            root(1)
            sa.wait_ge(mod_ready, 1)
            modulate(0, mul1, 0)
            sa.wait_ge(proj_done, 1)
            act_(qraw, ps[0][:], ACT.Copy).then_inc(q_raw_ready, 1)
            sa.wait_ge(va_done, 1)
            act_(vA.rearrange("p a b -> p (a b)"), ps[1][:], ACT.Copy).then_inc(va_ready, 1)
            sa.wait_ge(rope_ready, 1)

            with sa.Fori(0, PAIRS) as i:
                sa.wait_ge(proj_done, i * 4 + 2)
                act_(qraw, ps[0][:], ACT.Copy, scale=HD ** -0.5).then_inc(q_raw_ready, 1)
                for c, dst in ((1, qB), (2, kB), (3, vB.rearrange("p a b -> p (a b)"))):
                    sa.wait_ge(proj_done, i * 4 + (2 + c))
                    act_(dst, ps[c][:], ACT.Copy, scale=HD ** -0.5 if c == 1 else 1.0).then_inc(evac_done, 1)
                for a in range(2):
                    for b in range(4):
                        sa.wait_ge(sb_scored, i * 8 + (a * 4 + b + 1))
                        act_(spl[:, b, b * P:T], ps[4 + b][:, b * P:T], ACT.Abs).then_inc(abs_ready, 1)
                    for b in range(4):
                        sa.wait_ge(abs_ready, i * 8 + (a * 4 + b + 1))
                        act_(spl[:, b, b * P:T], spl[:, b, b * P:T], ACT.Exp, scale=-1.0).then_inc(act_steps, 1)
                    sa.wait_ge(max_ready, i * 2 + (a + 1))
                    for t in range(TT):
                        act_(prob[:, t, :], ps[t // 2][:, (t % 2) * 256:(t % 2) * 256 + 256], ACT.Exp,
                             bias=mx[:, 4 + t:5 + t], accum_out=sk4[:, t:t + 1]).then_inc(swa_exp, 1)
                    act_(sk4[:, 4:8], mx[:, 4:8], ACT.Exp, bias=sml[:, bass.ds(i * 2 + (S_SINK + a), 1)]).then_inc(swa_exp, 1)
                    for b in range(4):
                        sa.wait_ge(act_steps, i * 8 + (a * 4 + b + 1))
                        act_(spl[:, b, b * P:T], spl[:, b, b * P:T], ACT.Ln, bias=1.0).then_inc(log_ready, 1)
                    sa.wait_ge(probT_done, i * 2 + (a + 1))
                    for c in range(2):
                        last = act_(probT[:, 2 * c:2 * c + 2, :].rearrange("p a b -> p (a b)"), ps[2 + c][:], ACT.Copy)
                    last.then_inc(probT_ready, 1)
                    for b in range(4):
                        sa.wait_ge(sb_summed, i * 8 + (a * 4 + b + 1))
                        act_(atB[:, b, b * P:T], ps[4 + b][:, b * P:T], ACT.Exp).then_inc(at_ready, 1)

            with sa.Fori(0, DC // 2) as r:
                for s in range(2):
                    sa.wait_ge(merged_ready, r * 2 + FREE)
                    for c, dst in enumerate((siga, sigb)):
                        sa.wait_ge(gate_done, r * 4 + (s * 2 + c + 1))
                        act_(dst[:, s, :], ps[4 * s + c][:], ACT.Sigmoid).then_inc(sig_ready, 1)
            sa.wait_ge(x_ready, DC)
            squares(DC, squares2)
            root(2)
            sa.wait_ge(mod_ready, 2)
            modulate(1, mul2, 3)
            for k in range(DC):
                sa.wait_ge(h_ready, DC + k + 1)
                act_(hs[:, 0, k, :], h[:, k, :], ACT.Copy).then_inc(hi_ready, 1)
            with sa.Fori(0, HEADS) as i:
                sa.wait_ge(score_done, i * 2 + FREE)
                for c in range(2):
                    sa.wait_ge(qry_done, i * 2 + (c + 1) + FREE)
                    act_(qv[:, c, :], ps[c][:], ACT.Copy).then_inc(qry_ready, 1)
                sa.wait_ge(score_used, i + FREE)
                for c in range(2):
                    sa.wait_ge(score_done, i * 2 + (c + 1) + FREE)
                    act_(sc[:, c, :, :].rearrange("p a b -> p (a b)"), ps[2 + c][:], ACT.Copy).then_inc(score_ready, 1)
                sa.wait_ge(best_ready, i + 1)
                act_(bv.rearrange("p a b -> p (a b)"), bv.rearrange("p a b -> p (a b)"), ACT.Exp).then_inc(best_exp, 1)
            for f in range(3):
                sa.wait_ge(slotsT_done, f + 1)
                act_(slotsT[:, f, :], ps[f][:], ACT.Copy).then_inc(slotsT_ready, 1)
            with sa.Fori(0, T // 128) as q:
                for c in range(2):
                    sa.wait_ge(g_out[c], q * 16 + FREE)
                    with sa.Fori(0, 8) as r:
                        for b in range(2):
                            sa.wait_ge(hot_done[b], q * 16 + r + (8 * c + 1) + FREE)
                            act_(stages[c][:, :, bass.ds(r * 8 + b * 4, 4)],
                                 ps[b][:].rearrange("p (t i) -> p i t", t=4), ACT.Copy).then_inc(staged[b], 1)
            def u_high(g, e):
                sa.wait_ge(u_in[e], g * 16 + 16)
                act_(us[:, e, 0, :], ut[:, e, :], ACT.Copy).then_inc(u_hi, 1)

            def v_high(g):
                sa.wait_ge(v_done, g * DC + FREE)
                for e in range(EG):
                    sa.wait_ge(v_in[e], g * 16 + 16)
                    act_(vs[:, 0, e * D:(e + 1) * D], vt[:, e * D:(e + 1) * D], ACT.Copy).then_inc(v_hi, 1)

            def gelus(g, split_next=True):
                for e in range(EG):
                    sa.wait_ge(s_done, g * EG + (e + 1))
                    if not isinstance(g, int) or g > 0:
                        sa.wait_ge(w_ready, (g - 1) * EG + (e + 1))
                    act_(gel[:, e, :], ps[e % 2][:], ACT.Gelu).then_inc(gelu_ready, 1)
                    if split_next:
                        u_high(g + 1, e)

            for e in range(EG):
                u_high(0, e)
            gelus(0)
            with sa.Fori(1, GROUPS - 1) as g:
                v_high(g - 1)
                gelus(g)
            v_high(GROUPS - 2)
            gelus(GROUPS - 1, False)
            v_high(GROUPS - 1)
            sa.wait_ge(x_ready, 2 * DC)
            squares(2 * DC, gel)
            root(3)

        @block.vector
        def _(ve):
            start(ve, *ring_free, oa_out, ob_out, merged_ready, score_used, acc_ready)
            nv = nc.vector
            step = Steps(ve, dve_steps)
            step.pad = pad[:]

            def inv_rms(n):
                ve.wait_ge(sq_summed, n * DC)
                nv.tensor_scalar(var[:], ps[7][:], 1.0 / D, EPS, ALU.mult, ALU.add).then_inc(var_ready, 1)
                ve.wait_ge(root_ready, n)
                step(nv.reciprocal(rstd[:], rstd[:]))

            def ada_product(n, slot, b, loads):
                ve.wait_ge(ring_in[slot], loads * 16)
                if not isinstance(n, int) or n >= 2:
                    ve.wait_ge(ada_summed, n - 1)
                w = ring[:, slot, :].rearrange("p (k n) -> p k n", k=DC)
                step(nv.tensor_scalar(adap[:, b, :], w[:, 0, :], cact[:, 0:1], None, ALU.mult))
                for k in range(1, DC):
                    ins = nv.scalar_tensor_tensor(adap[:, b, :], w[:, k, :], cact[:, k:k + 1], adap[:, b, :], ALU.mult, ALU.add)
                    if k < DC - 1:
                        step(ins)
                ins.then_inc(ada_ready, 1)
                ve.wait_ge(ada_ready, n + 1)
                ve.sem_inc(ring_free[slot], 1)

            ve.wait_ge(smalls_in, 48)
            step(nv.tensor_copy(turn, ang.bitcast(I32)))
            step(nv.tensor_scalar(ang, turn, cst[:, K_INV:K_INV + 1], None, ALU.mult))
            for dst, quarter in ((sinT, 0.0), (cosT, 0.25)):
                step(nv.tensor_scalar(turn, ang, 1 / TWO_PI, quarter, ALU.mult, ALU.add))
                step(nv.tensor_scalar(turn, turn, MAGIC, None, ALU.add))
                step(nv.tensor_scalar(turn, turn, -MAGIC, None, ALU.add))
                step(nv.scalar_tensor_tensor(dst, turn, -C1, ang, ALU.mult, ALU.add))
                step(nv.scalar_tensor_tensor(dst, turn, -C2, dst, ALU.mult, ALU.add))
                step(nv.scalar_tensor_tensor(dst, turn, -C3, dst, ALU.mult, ALU.add))
                step(nv.tensor_scalar(dst, dst, quarter * TWO_PI, None, ALU.add))
                nv.tensor_scalar(dst, dst, -3.1415925, 3.1415925, ALU.max, ALU.min).then_inc(angle_ready, 1)
            inv_rms(1)
            for k in range(DC):
                ve.wait_ge(x_in, 16)
                nv.tensor_tensor(h[:, k, :], x[:, k, :], rstd[:], ALU.mult).then_inc(norm_part, 1)
            ve.wait_ge(cact_ready, 1)
            for n in range(4):
                ada_product(n, n, n % 2, 1)
            ve.wait_ge(ada_summed, 4)
            step(nv.tensor_tensor(mod[:, 0:16], ps[6][:, 0:16], sml[:, S_B:S_B + 16], ALU.add))
            nv.scalar_tensor_tensor(mul1[:], part(1), 1.0, sml[:, S_G1:S_G1 + DC], ALU.add, ALU.mult).then_inc(mod_ready, 1)

            def rope(n, dst):
                ve.wait_ge(q_raw_ready, n)
                step(nv.tensor_tensor(dst, qraw, cosT, ALU.mult))
                ve.wait_ge(rot_done, n)
                step(nv.tensor_tensor(ang, ps[4][:], sinT, ALU.mult))
                nv.tensor_tensor(dst, dst, ang, ALU.add).then_inc(rope_ready, 1)

            ve.wait_ge(trig_ready, 2)
            rope(1, kR)

            with ve.Fori(0, PAIRS) as i:
                step.enter(i, 24)
                for a in range(2):
                    ada_product(i * 2 + (4 + a), a, a, i + 2)
                rope(i + 2, qR)
                for a in range(2):
                    lo, hi = a * HD, (a + 1) * HD
                    ve.wait_ge(swa_scored, i * 2 + (a + 1))
                    for c in range(2):
                        ins = nv.tensor_reduce(mx[:, 2 * c:2 * c + 2], ps[c][:].rearrange("p (a b) -> p a b", a=2), AX.X, ALU.max)
                    step(ins)
                    nv.tensor_scalar(mx[:, 4:8], mx[:, 0:4], sml[:, bass.ds(i * 2 + (S_SINK + a), 1)], -1.0,
                                     ALU.max, ALU.mult).then_inc(max_ready, 1)
                    ve.wait_ge(swa_exp, i * 10 + (a * 5 + 5))
                    step(nv.tensor_tensor(sk4[:, 8:12], sk4[:, 0:4], sk4[:, 4:8], ALU.add))
                    step(nv.reciprocal(sk4[:, 12:16], sk4[:, 8:12]))
                    for t in range(TT):
                        ins = nv.tensor_scalar(prob[:, t, :], prob[:, t, :], sk4[:, 12 + t:13 + t], None, ALU.mult)
                    ins.then_inc(prob_ready, 1)
                    for b in range(4):
                        ve.wait_ge(log_ready, i * 8 + (a * 4 + b + 1))
                        ins = nv.scalar_tensor_tensor(spl[:, b, b * P:T], ps[4 + b][:, b * P:T], 0.0, spl[:, b, b * P:T],
                                                      ALU.max, ALU.add)
                    step(ins)
                    for b in range(4):
                        nv.tensor_tensor(spl[:, b, b * P:(b + 1) * P], spl[:, b, b * P:(b + 1) * P], cst[:, K_CAUS:K_CAUS + P],
                                         ALU.mult).then_inc(sp_ready, 1)
                    ve.wait_ge(oa_done, i * 2 + (a + 1))
                    nv.tensor_copy(yA[lo:hi, bass.ds(i, 1), :].rearrange("p a n -> p (a n)"), ps[0][lo:hi, :]).then_inc(oa_out, 1)
                    ve.wait_ge(ob_done, i * 2 + (a + 1))
                    nv.tensor_copy(yB[lo:hi, bass.ds(i, 1), :].rearrange("p a n -> p (a n)"), ps[1][lo:hi, :]).then_inc(ob_out, 1)
                step.leave(PAIRS)

            ve.wait_ge(ada_summed, 12)
            step(nv.tensor_tensor(mod[:, 16:48], ps[7][:, 0:32], sml[:, S_B + 16:S_B + 48], ALU.add))
            nv.scalar_tensor_tensor(mul2[:], part(4), 1.0, sml[:, S_G2:S_G2 + DC], ALU.add, ALU.mult).then_inc(mod_ready, 1)
            with ve.Fori(0, DC // 2) as r:
                step.enter(r, 2)
                for s in range(2):
                    ve.wait_ge(sig_ready, r * 4 + (s * 2 + 2))
                    ve.wait_ge(up_done, r * 2 + (s + 1))
                    nv.tensor_tensor(ma[:, s, :], siga[:, s, :], ps[4 * s + 2][:], ALU.mult)
                    step(nv.tensor_tensor(mb[:, s, :], sigb[:, s, :], ps[4 * s + 3][:], ALU.mult))
                    nv.tensor_tensor(merged[:, bass.ds(r * 2 + s, 1), :].rearrange("p a n -> p (a n)"),
                                     ma[:, s, :], mb[:, s, :], ALU.add).then_inc(merged_ready, 1)
                step.leave(DC // 2)
            for m in range(DC):
                ve.wait_ge(out_done, m + 1)
                nv.scalar_tensor_tensor(x[:, m, :], ps[m % 2][:], part(2, m), x[:, m, :], ALU.mult, ALU.add).then_inc(x_ready, 1)
            inv_rms(2)
            for k in range(DC):
                nv.tensor_tensor(h[:, k, :], x[:, k, :], rstd[:], ALU.mult).then_inc(norm_part, 1)

            for k in range(DC):
                ve.wait_ge(hi_ready, k + 1)
                nv.tensor_tensor(hs[:, 1, k, :], h[:, k, :], hs[:, 0, k, :].bitcast(F32), ALU.subtract).then_inc(h_split, 1)

            with ve.Fori(0, HEADS) as i:
                step.enter(i, 13)
                step.wait_apart(score_ready, i * 2 + 2 + FREE)
                every = [(c, t) for c in range(2) for t in range(TT)]

                for c, t in every:
                    ins = nv.max(tv[:, c, t, 0:8], sc[:, c, t, :])
                step(ins, apart=True)
                for c, t in every:
                    nv.max_index(ti[:, c, t, 0:8], tv[:, c, t, 0:8], sc[:, c, t, :])
                    ins = nv.match_replace(sc2[:, c, t, :], tv[:, c, t, 0:8], sc[:, c, t, :], LOWEST)
                ins.then_inc(score_used, 1)
                step.wait_apart(score_used, i + 1 + FREE)
                for c, t in every:
                    ins = nv.max(tv[:, c, t, 8:16], sc2[:, c, t, :])
                step(ins, apart=True)
                for c, t in every:
                    nv.max_index(ti[:, c, t, 8:16], tv[:, c, t, 8:16], sc2[:, c, t, :])
                for t in range(TT):
                    ins = nv.tensor_tensor(cand[:, t, :].rearrange("p (a b) -> p a b", a=TOPK),
                                           tv[:, 0, t, :].unsqueeze(2).to_broadcast([P, TOPK, TOPK]),
                                           tv[:, 1, t, :].unsqueeze(1).to_broadcast([P, TOPK, TOPK]), ALU.add)
                step(ins, apart=True)
                for t in range(TT):
                    ins = nv.max(bv[:, t, 0:8], cand[:, t, :])
                step(ins, apart=True)
                for t in range(TT):
                    nv.max_index(bi[:, t, 0:8], bv[:, t, 0:8], cand[:, t, :])
                    ins = nv.match_replace(cand2[:, t, :], bv[:, t, 0:8], cand[:, t, :], LOWEST)
                step(ins, apart=True)
                for t in range(TT):
                    ins = nv.max(bv[:, t, 8:16], cand2[:, t, :])
                step(ins, apart=True)
                for t in range(TT):
                    ins = nv.max_index(bi[:, t, 8:16], bv[:, t, 8:16], cand2[:, t, :])
                nv.tensor_copy(den[:, 0:TT], bv[:, :, 0:1].rearrange("p a b -> p (a b)"))
                step(nv.tensor_copy(tif.rearrange("p a b c -> p (a b c)"), ti.rearrange("p a b c -> p (a b c)")))
                nv.tensor_tensor(bv, bv, den[:, 0:TT].unsqueeze(2).to_broadcast([P, TT, TOPK]), ALU.subtract).then_inc(best_ready, 1)
                bif = bi.rearrange("p a b -> p (a b)")
                nv.tensor_scalar(bij[:, 0, :], bif, 4, None, ALU.logical_shift_right)
                step(nv.tensor_scalar(bij[:, 1, :], bif, 15, None, ALU.bitwise_and))
                step(nv.tensor_copy(bijf.rearrange("p a b -> p (a b)"), bij.rearrange("p a b -> p (a b)")))
                for c in range(2):
                    ins = nv.tensor_tensor(pick[:, c, :, :], bijf[:, c, :].unsqueeze(2).to_broadcast([P, TT * TOPK, TOPK]),
                                           cst[:, K_IOTA:K_IOTA + TOPK].unsqueeze(1).to_broadcast([P, TT * TOPK, TOPK]), ALU.is_equal)
                step(ins)
                for c in range(2):
                    p4 = pick[:, c, :, :].rearrange("p (t s) k -> p t s k", t=TT)
                    ins = nv.tensor_tensor(p4, p4, tif[:, c, :, :].unsqueeze(2).to_broadcast([P, TT, TOPK, TOPK]), ALU.mult)
                step(ins)
                for c in range(2):
                    nv.tensor_reduce(slots[:, c, :, bass.ds(i * TOPK, TOPK)], pick[:, c, :, :].rearrange("p (t s) k -> p t s k", t=TT),
                                     AX.X, ALU.add).then_inc(slots_ready, 1)
                ve.wait_ge(best_exp, i + 1)
                step(nv.tensor_reduce(den[:, 0:TT], bv, AX.X, ALU.add))
                step(nv.reciprocal(den[:, TT:2 * TT], den[:, 0:TT]))
                nv.tensor_tensor(slots[:, 2, :, bass.ds(i * TOPK, TOPK)], bv, den[:, TT:2 * TT].unsqueeze(2).to_broadcast([P, TT, TOPK]),
                                 ALU.mult).then_inc(slots_ready, 1)
                step.leave(HEADS)

            ve.wait_ge(slotsT_ready, 3)
            with ve.Fori(0, T // 8) as r:
                for b in range(2):
                    ve.wait_ge(hot_done[b], r + FREE)
                    for q in range(4):
                        def col(f):
                            return slotsT[:, f, bass.ds(r * 8 + (b * 4 + q), 1)]
                        nv.tensor_scalar(ohi[:, b, q, :], cst[:, K_IOTA:K_IOTA + P], col(0), None, ALU.is_equal).then_inc(hot_ready[b], 1)
                        nv.tensor_scalar(ohj[:, b, q, :], cst[:, K_IOTA:K_IOTA + P], col(1), col(2), ALU.is_equal, ALU.mult).then_inc(hot_ready[b], 1)

            ve.wait_ge(qry_done, 2 * HEADS + FREE)
            nv.memset(acc, 0.0).then_inc(acc_zero, 1)
            ve.wait_ge(acc_zero, 1)

            def u_low(g, e):
                ve.wait_ge(u_hi, g * EG + (e + 1))
                nv.tensor_tensor(us[:, e, 1, :], ut[:, e, :], us[:, e, 0, :].bitcast(F32), ALU.subtract).then_inc(u_split, 1)

            def weigh(g):
                for e in range(EG):
                    b = e % 2
                    ve.wait_ge(gelu_ready, g * EG + (e + 1))
                    ve.wait_ge(g_in[b], g * 32 + (16 * (e // 2) + 16))
                    nv.tensor_tensor(wg_[:, b, :], gel[:, e, :], gt[:, b, :], ALU.mult).then_inc(w_ready, 1)
                    v = slice(e * D, (e + 1) * D)
                    ve.wait_ge(v_hi, g * EG + (e + 1))
                    nv.tensor_tensor(vs[:, 1, v], vt[:, v], vs[:, 0, v].bitcast(F32), ALU.subtract).then_inc(v_split, 1)
                    ve.wait_ge(w_ready, g * EG + (e + 1))
                    nv.tensor_copy(ar[:, e, 0, :], wg_[:, b, :]).then_inc(a_hi, 1)
                    ve.wait_ge(a_hi, g * EG + (e + 1))
                    nv.tensor_tensor(ar[:, e, 1, :], wg_[:, b, :], ar[:, e, 0, :].bitcast(F32), ALU.subtract).then_inc(a_split, 1)

            def add(g):
                if not isinstance(g, int) or g > 0:
                    ve.wait_ge(acc_ready, g * DC + FREE)
                for k in range(DC):
                    ve.wait_ge(v_done, g * DC + (k + 1 + FREE))
                    nv.tensor_tensor(acc[:, k, :], acc[:, k, :], ps[4 + k % 4][:], ALU.add).then_inc(acc_ready, 1)

            for g in range(2):
                for e in range(EG):
                    u_low(g, e)
            with ve.Fori(1, GROUPS - 1) as g:
                weigh(g - 1)
                for e in range(EG):
                    u_low(g + 1, e)
                add(g - 1)
            weigh(GROUPS - 2)
            add(GROUPS - 2)
            weigh(GROUPS - 1)
            add(GROUPS - 1)
            ve.wait_ge(acc_ready, GROUPS * DC + FREE)
            for k in range(DC):
                nv.scalar_tensor_tensor(x[:, k, :], acc[:, k, :], part(5, k), x[:, k, :], ALU.mult, ALU.add).then_inc(x_ready, 1)
            inv_rms(3)
            ve.wait_ge(x_ready, 2 * DC)
            for k in range(DC):
                nv.scalar_tensor_tensor(h[:, k, :], x[:, k, :], sml[:, S_GF + k:S_GF + k + 1], rstd[:], ALU.mult, ALU.mult).then_inc(y_ready, 1)


def constants():
    k = np.zeros((P, K_END), np.float32)
    p, f = np.arange(P)[:, None], np.arange(P)[None, :]
    k[:, K_ID:K_ID + P] = p == f
    k[:, K_ONE:K_ONE + P] = 1.0
    k[:, K_NTRI:K_NTRI + P] = np.where(p >= f, -1.0, 0.0)
    k[:, K_NONE:K_NONE + P] = -1.0
    k[:, K_SBM:K_SBM + P] = np.where(p >= f, BIG, 0.0)
    k[:, K_CAUS:K_CAUS + P] = p < f
    half = HD // 2
    for m in range(P):
        if m % HD < half:
            k[m + half, K_ROT + m] = -1.0
        else:
            k[m - half, K_ROT + m] = 1.0
    k[:, K_IOTA:K_IOTA + P] = f
    q, c = np.arange(P)[:, None] // HD, np.arange(2 * P)[None, :] // HD - 2
    ok = (c == q) | (c == q - 1)
    k[:, K_SWA:K_SWA + 256] = np.where(ok, 0.0, BIG)
    k[:, K_SWA0:K_SWA0 + 256] = np.where(ok & (c >= 0), 0.0, BIG)
    k[:, K_INV] = np.float32(10000.0) ** (-(np.arange(P) % half).astype(np.float32) / np.float32(half))
    return k


def kernel(x, c, positions, norm1_g, norm2_g, final_g, w_ada, b_ada, w_in, sinks,
           w_up_swa, w_up_sb, w_out, w_query, sub_keys, expert_u, expert_v):
    import concourse.bacc as bacc
    from concourse.bass_utils import run_bass_kernel_spmd

    def columns(v):
        return np.asarray(v).reshape(-1, P).T

    def tiles(w):
        w = np.asarray(w)
        return w.reshape(w.shape[0] // P, P, w.shape[1]).transpose(1, 0, 2)

    order = np.array([h * HD + d for i in range(PAIRS) for h in (i, i + PAIRS) for d in range(HD)])
    pair_sinks = np.asarray(sinks)[0][[h for i in range(PAIRS) for h in (i, i + PAIRS)]]
    small = np.concatenate([columns(c[0]), columns(norm1_g[0]), columns(norm2_g[0]), columns(final_g),
                            columns(b_ada[0]), np.repeat(pair_sinks[None], P, 0)], 1)
    wi = np.asarray(w_in)[0]
    qa, kv, qb, kb, vb, g = (wi[:, 0:512][:, order], wi[:, 512:768], wi[:, 768:1280], wi[:, 1280:1792],
                             wi[:, 1792:2304], wi[:, 2304:])
    pair = np.stack([tiles(np.concatenate([w[:, i * P:(i + 1) * P] for w in (qa, qb, kb, vb)], 1)).reshape(P, -1)
                     for i in range(PAIRS)])
    gate = np.stack([tiles(np.concatenate([g[:, m * P:(m + 1) * P], g[:, D + m * P:D + (m + 1) * P]], 1)).reshape(P, -1)
                     for m in range(DC)])
    ups = np.concatenate([np.asarray(w_up_swa)[0][order], np.asarray(w_up_sb)[0]], 0)
    up = np.stack([tiles(ups[:, m * P:(m + 1) * P]).reshape(P, -1) for m in range(DC)])
    wo = np.asarray(w_out)[0]
    out = np.stack([tiles(wo[:, m * P:(m + 1) * P]).reshape(P, -1) for m in range(DC)])
    wq = np.asarray(w_query)[0]
    qry = np.stack([tiles(wq[:, m * 256:(m + 1) * 256]).reshape(P, -1) for m in range(HEADS)])
    wa = np.asarray(w_ada)[0]
    ada = np.stack([tiles(wa[:, m * 512:(m + 1) * 512]).reshape(P, -1) for m in range(12)])
    skT = np.asarray(sub_keys)[0].reshape(2 * HEADS, NK, P).transpose(2, 0, 1)
    eu = np.asarray(expert_u)[0].reshape(NK, P, DC, P).transpose(0, 3, 2, 1).reshape(NK, P, DC * P)
    arrays = {
        "xT": tiles(np.asarray(x)[0].T), "small": small, "consts": constants(), "pos": np.asarray(positions),
        "w_ada": ada, "w_kava": tiles(kv), "w_pair": pair, "w_gate": gate, "w_up": up, "w_out": out, "w_qry": qry,
        "skT": skT, "euT": eu, "ev": np.asarray(expert_v)[0].reshape(NK, P, D),
    }
    nc = bacc.Bacc("TRN2", target_bir_lowering=False, num_devices=1)
    arrays = {k: np.ascontiguousarray(a) for k, a in arrays.items()}
    args = [nc.dram_tensor(k, a.shape, mybir.dt.from_np(a.dtype), kind="ExternalInput").ap() for k, a in arrays.items()]
    args.append(nc.dram_tensor("outT", (P, DC, T), F32, kind="ExternalOutput").ap())
    build(nc, *args)
    got = run_bass_kernel_spmd(nc, [arrays], core_ids=[0]).results[0]["outT"]
    return np.ascontiguousarray(got.transpose(2, 1, 0)).reshape(1, T, D)
```

```python
from contextlib import ExitStack

import numpy as np
import concourse.bass as bass
from concourse import mybir

P = 128
T = 512
D = 1024
TT = T // P
DC = D // P
NMOD = 6
HD = 64
PAIRS = 4
HEADS = 8
TOPK = 16
NK = 128
RING = 4
EARLY = 8
WITH_G = T // 8
ADA = (5, 5, 1, 1)
FREE = 1
EPS = 1e-6
BIG = -1e30
LOWEST = -3.0e38
MAGIC = 12582912.0
TWO_PI = 2 * np.pi
C1 = 6.28125
C2 = float(np.float32(1935.0 * 2.0 ** -20))
C3 = float(TWO_PI - C1 - C2)

ALU = mybir.AluOpType
ACT = mybir.ActivationFunctionType
F32 = mybir.dt.float32
F32R = mybir.dt.float32r
U32 = mybir.dt.uint32
I32 = mybir.dt.int32
AX = mybir.AxisListType

(K_ID, K_ONE, K_NTRI, K_NONE, K_SBM, K_CAUS, K_ROT, K_IOTA, K_SWA0, K_SWA, K_INV, K_END) = (
    0, 128, 256, 384, 512, 640, 768, 896, 1024, 1280, 1536, 1537)
S_C, S_G1, S_G2, S_GF, S_B, S_SINK, S_END = 0, 8, 16, 24, 32, 80, 88


class Steps:

    def __init__(self, engine, sem):
        self.engine, self.sem, self.n, self.at = engine, sem, 0, 0

    def __call__(self, instruction, apart=False):
        instruction.then_inc(self.sem, 1)
        self.n += 1
        if apart:
            self.wait_apart(self.sem, self.at + self.n)
        else:
            self.engine.wait_ge(self.sem, self.at + self.n)

    def wait_apart(self, sem, value):
        self.engine.wait_ge(sem, value)
        self.engine.memset(self.pad, 0.0)

    def enter(self, i, per_turn):
        self.before, self.per = self.n, per_turn
        self.at, self.n = i * per_turn + self.before, 0

    def leave(self, turns):
        assert self.n == self.per, (self.n, self.per)
        self.at, self.n = 0, self.before + turns * self.per


def row(a, i):
    return a[bass.ds(i, 1), :, :].rearrange("a p n -> p (a n)")


def build(nc, xT, small, consts, pos, w_ada, w_kava, w_pair, w_gate, w_up, w_out, w_qry, skT, euT, ev, outT):
    with ExitStack() as ctx:
        def sb(name, shape, dt=F32):
            return ctx.enter_context(nc.sbuf_tensor(name, shape, dt))

        def sem(name):
            return ctx.enter_context(nc.semaphore(name))

        ps = [ctx.enter_context(nc.psum_tensor(f"bank{n}", [P, 512], F32)) for n in range(8)]
        gelu_dram = nc.dram_tensor("gelu_scratch", (NK, P, T), F32, kind="Internal").ap()
        gates_dram = nc.dram_tensor("gates_scratch", (NK, P, T), F32, kind="Internal").ap()

        cst = sb("cst", [P, K_END])
        sml = sb("sml", [P, S_END])
        x = sb("x", [P, DC, T])
        h = sb("h", [P, DC, T])
        mod = sb("mod", [P, NMOD * DC])
        mul1 = sb("mul1", [P, DC])
        mul2 = sb("mul2", [P, DC])
        cact = sb("cact", [P, DC])
        var = sb("var", [P, T])
        rstd = sb("rstd", [P, T])
        pad = sb("pad", [P, 1])
        ident = cst[:, K_ID:K_ID + P]
        ones = cst[:, K_ONE:K_ONE + P]

        def part(m, k=None):
            return mod[:, m * DC:(m + 1) * DC] if k is None else mod[:, m * DC + k:m * DC + k + 1]

        ARENA = 164 * 256
        arena_at = -(-nc.sbuf_base // 64) * 64
        arena = nc.alloc_sbuf_tensor_at("arena", [P, ARENA], F32, offset=arena_at)
        top = [0]

        def carve(*shape, split=None):
            n = int(np.prod(shape))
            if split:
                a = nc.alloc_sbuf_tensor_at(split, [P, n], F32R, offset=arena_at + 4 * top[0])[:]
            else:
                a = arena[:, top[0]:top[0] + n]
            top[0] += n
            assert top[0] <= ARENA, top[0]
            if len(shape) == 2:
                a = a.rearrange("p (a b) -> p a b", a=shape[0])
            if len(shape) == 3:
                a = a.rearrange("p (a b c) -> p a b c", a=shape[0], b=shape[1])
            return a

        ring = carve(4, 4096)
        front = top[0]
        pairw = carve(DC, 512)
        kavaw = pairw[:, :, 0:256]
        cosT = carve(T)
        sinT = carve(T)
        ang = carve(T)
        turn = carve(T)
        kR = carve(T)
        vA = carve(TT, P)
        qraw = carve(T)
        qR = carve(T)
        qB = carve(T)
        kB = carve(T)
        vB = carve(TT, P)
        prob = carve(TT, 256)
        probT = carve(TT, 256)
        spl = carve(4, T)
        atB = carve(4, T)
        adap = carve(2, T)
        mx = carve(8)
        sk4 = carve(16)
        att_end = top[0]
        top[0] = front
        siga = carve(2, T)
        sigb = carve(2, T)
        ma = carve(2, T)
        mb = carve(2, T)
        merged = carve(DC, T)
        yA = arena[:, ARENA - 2 * PAIRS * T:ARENA - PAIRS * T].rearrange("p (a b) -> p a b", a=PAIRS)
        yB = arena[:, ARENA - PAIRS * T:ARENA].rearrange("p (a b) -> p a b", a=PAIRS)
        assert max(top[0], att_end) <= ARENA - 2 * PAIRS * T, (top[0], att_end)
        squares2 = yB[:, 2:4, :]
        top[0] = 0
        stages = (carve(NK, 64), carve(NK, 64))
        ohi = carve(2, 4, P)
        ohj = carve(2, 4, P)
        slotsT = carve(3, T)
        top_k_at = top[0]
        skt = carve(2 * HEADS, P)
        qv = carve(2, T)
        sc = carve(2, TT, P)
        sc2 = carve(2, TT, P)
        tv = carve(2, TT, TOPK)
        ti = carve(2, TT, TOPK).bitcast(U32)
        tif = carve(2, TT, TOPK)
        cand = carve(TT, 256)
        cand2 = carve(TT, 256)
        bv = carve(TT, TOPK)
        bi = carve(TT, TOPK).bitcast(U32)
        bij = carve(2, TT * TOPK).bitcast(U32)
        bijf = carve(2, TT * TOPK)
        pick = carve(2, TT * TOPK, TOPK)
        den = carve(2 * TT)
        slots = carve(3, TT, P)
        top_k_end = top[0]
        top[0] = 0
        ute = carve(2, DC * P)
        gele = carve(2, T)
        assert top[0] <= 2 * 4096
        top[0] = top_k_at
        ut = carve(RING, DC * P)
        us = carve(2, 2, DC * P, split="u_split")
        gel = carve(RING, T)
        top[0] = max(top[0], top_k_end)
        hs = carve(2 * DC, T, split="h_split").rearrange("p (s k) n -> p s k n", s=2)
        top[0] = 0
        vt = carve(RING, D)
        vs = carve(2, 2, D, split="v_split")
        gl = carve(RING, T)
        gt = carve(RING, T)
        wgt = carve(2, T)
        ar = carve(2, 2, T, split="a_split")
        assert top[0] <= top_k_at
        squares3 = wgt

        smalls_in, x_in, kava_in, pair_in, sk_in = map(sem, ("smalls_in", "x_in", "kava_in", "pair_in", "sk_in"))
        ring_in = [sem(f"ring_in{s}") for s in range(4)]
        ring_free = [sem(f"ring_free{s}") for s in range(4)]
        ada_ready, ada_summed = sem("ada_ready"), sem("ada_summed")
        hi_ready, h_split, u_hi, u_split, v_hi, v_split, a_split = map(sem, (
            "hi_ready", "h_split", "u_hi", "u_split", "v_hi", "v_split", "a_split"))
        cact_ready, mod_ready = sem("cact_ready"), sem("mod_ready")
        sq_ready, sq_summed, var_ready, root_ready, norm_part, h_ready = map(sem, (
            "sq_ready", "sq_summed", "var_ready", "root_ready", "norm_part", "h_ready"))
        dve_steps, act_steps = sem("dve_steps"), sem("act_steps")
        angle_ready, trig_ready = sem("angle_ready"), sem("trig_ready")
        proj_done, q_raw_ready, rot_done, rope_ready, evac_done = map(sem, (
            "proj_done", "q_raw_ready", "rot_done", "rope_ready", "evac_done"))
        va_done, va_ready = sem("va_done"), sem("va_ready")
        swa_scored, max_ready, swa_exp, prob_ready, probT_done, probT_ready, oa_done, oa_out = map(sem, (
            "swa_scored", "max_ready", "swa_exp", "prob_ready", "probT_done", "probT_ready", "oa_done", "oa_out"))
        sb_scored, abs_ready, log_ready, sp_ready, sb_summed, at_ready, ob_done, ob_out = map(sem, (
            "sb_scored", "abs_ready", "log_ready", "sp_ready", "sb_summed", "at_ready", "ob_done", "ob_out"))
        gate_done, sig_ready, up_done, merged_ready = map(sem, ("gate_done", "sig_ready", "up_done", "merged_ready"))
        out_done, x_ready = sem("out_done"), sem("x_ready")
        qry_done, qry_ready, score_done, score_ready, score_used = map(sem, (
            "qry_done", "qry_ready", "score_done", "score_ready", "score_used"))
        best_ready, best_exp, slots_ready, slotsT_done, slotsT_ready = map(sem, (
            "best_ready", "best_exp", "slots_ready", "slotsT_done", "slotsT_ready"))
        hot_ready = [sem("hot_ready0"), sem("hot_ready1")]
        hot_done = [sem("hot_done0"), sem("hot_done1")]
        staged = [sem("staged0"), sem("staged1")]
        g_out = [sem("g_out0"), sem("g_out1")]
        stage_free = [sem("stage_free0"), sem("stage_free1")]
        e_in = [sem(f"e_in{e}") for e in range(2)]
        u_in = [sem(f"u_in{e}") for e in range(RING)]
        v_in = [sem(f"v_in{e}") for e in range(RING)]
        g_in = [sem(f"g_in{e}") for e in range(RING)]
        e_out = [sem(f"e_out{e}") for e in range(2)]
        gelu_out = [sem(f"gelu_out{e}") for e in range(RING)]
        s_done, gelu_ready, w_ready, a_hi, v_done = map(sem, ("s_done", "gelu_ready", "w_ready", "a_hi", "v_done"))
        last_turn = (NK - EARLY) // RING - 1
        y_ready, y_out = sem("y_ready"), sem("y_out")

        def start(engine, *sems):
            for s in sems:
                engine.sem_inc(s, FREE)

        block = ctx.enter_context(nc.Block())

        @block.sync
        def _(sp):
            sp.dma_start(sml[:], small).then_inc(smalls_in, 16)
            sp.dma_start(cst[:], consts).then_inc(smalls_in, 16)
            sp.dma_start(ang.bitcast(I32), pos.to_broadcast([P, T])).then_inc(smalls_in, 16)
            sp.dma_start(x[:], xT).then_inc(x_in, 16)
            for n in range(4):
                sp.dma_start(ring[:, n, :], w_ada[n]).then_inc(ring_in[n], 16)
            sp.dma_start(kavaw, w_kava).then_inc(kava_in, 16)
            with sp.Fori(0, PAIRS) as i:
                for a in range(2):
                    sp.wait_ge(ring_free[a], i + 1 + FREE)
                    sp.dma_start(ring[:, a, :], row(w_ada, i * 2 + (4 + a))).then_inc(ring_in[a], 16)
            for m in range(DC):
                s = m % 4
                if m < 4:
                    sp.wait_ge(ring_free[s], ADA[s] + FREE)
                else:
                    sp.wait_ge(up_done, s + 1)
                sp.dma_start(ring[:, s, 0:2048], w_gate[m]).then_inc(ring_in[s], 16)
                sp.dma_start(ring[:, s, 2048:3072], w_up[m]).then_inc(ring_in[s], 16)
            for s in range(2):
                sp.wait_ge(up_done, 4 + s + 1)
                sp.dma_start(ring[:, s, :].rearrange("p (m n) -> p m n", m=4),
                             w_out[4 * s:4 * s + 4, :, :].rearrange("m p n -> p m n")).then_inc(ring_in[s], 16)
            sp.wait_ge(out_done, DC)
            sp.dma_start(skt, skT).then_inc(sk_in, 16)
            with sp.Fori(0, HEADS // 2) as r:
                sp.wait_ge(qry_done, r * 4 + FREE)
                sp.wait_ge(s_done, r * 2 + FREE)
                for s in range(2):
                    sp.dma_start(ring[:, 2 + s, 0:2048], row(w_qry, r * 2 + s)).then_inc(ring_in[2 + s], 16)
                    sp.dma_start(ute[:, s, :], row(euT, r * 2 + s)).then_inc(e_in[s], 16)

            sp.wait_ge(slotsT_ready, 3)
            for e in range(RING):
                sp.dma_start(ut[:, e, :], euT[EARLY + e]).then_inc(u_in[e], 16)
            with sp.Fori(1, (NK - EARLY) // RING) as r:
                for e in range(RING):
                    sp.wait_ge(u_split, r * RING + (e + 1 - RING))
                    sp.dma_start(ut[:, e, :], row(euT, r * RING + (EARLY + e))).then_inc(u_in[e], 16)
            for c in range(2):
                sp.wait_ge(g_out[c], 32 * (T // 128))

            def load_v(r, first):
                for e in range(RING):
                    n = r * RING + e
                    if not first:
                        sp.wait_ge(v_split, r * RING + (e + 1 - RING))
                    sp.dma_start(vt[:, e, :], row(ev, n)).then_inc(v_in[e], 16)
                    if not first:
                        sp.wait_ge(w_ready, r * RING + (e + 1 - RING))
                    sp.dma_start(gt[:, e, :], row(gates_dram, n)).then_inc(g_in[e], 16)
                    if first:
                        sp.wait_ge(e_out[e % 2], 16 * EARLY // 2 + FREE)
                    sp.dma_start(gl[:, e, :], row(gelu_dram, n)).then_inc(g_in[e], 16)

            load_v(0, True)
            load_v(1, False)
            with sp.Fori(2, NK // RING) as r:
                for e in range(RING):
                    sp.wait_ge(gelu_out[e], (r - 1) * 16 + FREE)
                load_v(r, False)
            sp.wait_ge(y_ready, DC)
            sp.dma_start(outT, h[:]).then_inc(y_out, 16)
            sp.wait_ge(y_out, 16)

        @block.gpsimd
        def _(pool):
            start(pool, *stage_free)
            pool.wait_ge(va_done, 1)
            with pool.Fori(0, PAIRS) as i:
                pool.wait_ge(proj_done, i * 4 + 1)
                pool.dma_start(pairw.rearrange("p k n -> p (k n)"), row(w_pair, i)).then_inc(pair_in, 16)
            with pool.Fori(0, T // 128) as q:
                for c in range(2):
                    for b in range(2):
                        pool.wait_ge(staged[b], q * 16 + (8 * c + 8) + FREE)
                    for i0 in range(0, NK, NK // 2):
                        pool.dma_start(gates_dram[i0:i0 + NK // 2, :, bass.ds(q * 128 + c * 64, 64)].rearrange("i j t -> j i t"),
                                       stages[c][:, i0:i0 + NK // 2, :]).then_inc(g_out[c], 16)
                    pool.wait_ge(g_out[c], q * 32 + 32)
                    pool.sem_inc(stage_free[c], 1)

        @block.tensor
        def _(pe):
            start(pe, *hot_done, qry_done, score_done, s_done, v_done)
            def rms_sum(first, squares):
                for k in range(DC):
                    pe.wait_ge(sq_ready, first + k + 1)
                    pe.matmul(ps[7][:], ones, squares[:, k % 2, :], start=(k == 0), stop=(k == DC - 1)).then_inc(sq_summed, 1)

            def ada_sum(n, b, bank, col):
                pe.wait_ge(ada_ready, n + 1)
                for m in range(4):
                    last = pe.matmul(bank[:, bass.ds(col + m, 1)], adap[:, b, m * P:(m + 1) * P], ones[:, 0:1], start=True, stop=True)
                last.then_inc(ada_summed, 1)

            rms_sum(0, spl)
            for n in range(4):
                ada_sum(n, n % 2, ps[6], n * 4)
            pe.wait_ge(h_ready, DC)
            pe.wait_ge(kava_in, 16)
            for k in range(DC):
                last = pe.matmul(ps[0][:], kavaw[:, k, 0:P], h[:, k, :], start=(k == 0), stop=(k == DC - 1))
            last.then_inc(proj_done, 1)
            for t in range(TT):
                for k in range(DC):
                    last = pe.matmul(ps[1][:, t * P:(t + 1) * P], h[:, k, t * P:(t + 1) * P], kavaw[:, k, P:2 * P],
                                     start=(k == 0), stop=(k == DC - 1))
            last.then_inc(va_done, 1)
            pe.wait_ge(q_raw_ready, 1)
            pe.matmul(ps[4][:], cst[:, K_ROT:K_ROT + P], qraw, start=True, stop=True).then_inc(rot_done, 1)
            pe.wait_ge(va_ready, 1)
            pe.wait_ge(rope_ready, 1)

            with pe.Fori(0, PAIRS) as i:
                pe.wait_ge(pair_in, i * 16 + 16)
                pe.wait_ge(oa_out, i * 2 + FREE)
                pe.wait_ge(ob_out, i * 2 + FREE)
                for c in range(3):
                    for k in range(DC):
                        last = pe.matmul(ps[c][:], pairw[:, k, c * P:(c + 1) * P], h[:, k, :], start=(k == 0), stop=(k == DC - 1))
                    last.then_inc(proj_done, 1)
                for t in range(TT):
                    for k in range(DC):
                        last = pe.matmul(ps[3][:, t * P:(t + 1) * P], h[:, k, t * P:(t + 1) * P], pairw[:, k, 3 * P:4 * P],
                                         start=(k == 0), stop=(k == DC - 1))
                last.then_inc(proj_done, 1)
                for a in range(2):
                    ada_sum(i * 2 + (4 + a), a, ps[7], i * 8 + 4 * a)
                pe.wait_ge(q_raw_ready, i + 2)
                pe.wait_ge(at_ready, i * 8 + FREE)
                pe.matmul(ps[4][:], cst[:, K_ROT:K_ROT + P], qraw, start=True, stop=True).then_inc(rot_done, 1)
                pe.wait_ge(evac_done, i * 3 + 3)
                pe.wait_ge(rope_ready, i + 2)
                for a in range(2):
                    lo, hi = a * HD, (a + 1) * HD
                    for t in range(TT):
                        at = ps[t // 2][:, (t % 2) * 256:(t % 2) * 256 + 256]
                        mask = cst[:, K_SWA0:K_SWA0 + 256] if t == 0 else cst[:, K_SWA:K_SWA + 256]
                        pe.matmul(at, ident, mask, start=True, stop=False)
                        if t == 0:
                            last = pe.matmul(at[:, P:2 * P], qR[lo:hi, 0:P], kR[lo:hi, 0:P], start=False, stop=True)
                        else:
                            last = pe.matmul(at, qR[lo:hi, t * P:(t + 1) * P], kR[lo:hi, (t - 1) * P:(t + 1) * P],
                                             start=False, stop=True)
                    last.then_inc(swa_scored, 1)
                    pe.wait_ge(at_ready, i * 8 + a * 4 + FREE)
                    for b in range(4):
                        pe.matmul(ps[4 + b][:, b * P:T], kB[lo:hi, b * P:(b + 1) * P], qB[lo:hi, b * P:T],
                                  start=True, stop=True).then_inc(sb_scored, 1)
                    pe.wait_ge(prob_ready, i * 2 + (a + 1))
                    for t in range(TT):
                        for c in range(2):
                            last = pe.transpose(ps[2 + t // 2][:, (t % 2) * 256 + c * P:(t % 2) * 256 + (c + 1) * P],
                                                prob[:, t, c * P:(c + 1) * P], ident)
                    last.then_inc(probT_done, 1)
                    pe.wait_ge(sp_ready, i * 8 + (a * 4 + 4))
                    for b in range(4):
                        pe.matmul(ps[4 + b][:, b * P:T], cst[:, K_NTRI:K_NTRI + P], spl[:, b, b * P:T], start=False, stop=False,
                                  skip_group_check=True)
                        for c in range(b + 1, 4):
                            pe.matmul(ps[4 + b][:, c * P:T], cst[:, K_NONE:K_NONE + P], spl[:, c, c * P:T], start=False, stop=False,
                                      skip_group_check=True)
                        pe.matmul(ps[4 + b][:, b * P:(b + 1) * P], ident, cst[:, K_SBM:K_SBM + P], start=False, stop=True,
                                  skip_group_check=True).then_inc(sb_summed, 1)
                    pe.wait_ge(probT_ready, i * 2 + (a + 1))
                    for t in range(TT):
                        for c in ((1,) if t == 0 else (0, 1)):
                            last = pe.matmul(ps[0][lo:hi, t * P:(t + 1) * P], vA[:, t - 1 + c, lo:hi],
                                             probT[:, t, c * P:(c + 1) * P], start=(c == 0 or t == 0), stop=(c == 1))
                    last.then_inc(oa_done, 1)
                    for b in range(4):
                        pe.wait_ge(at_ready, i * 8 + (a * 4 + b + 1) + FREE)
                        last = pe.matmul(ps[1][lo:hi, b * P:T], vB[:, b, lo:hi], atB[:, b, b * P:T], start=(b == 0), stop=(b == 3),
                                         skip_group_check=True)
                    last.then_inc(ob_done, 1)
                    if a == 0:
                        pe.wait_ge(oa_out, i * 2 + 1 + FREE)
                        pe.wait_ge(ob_out, i * 2 + 1 + FREE)

            pe.wait_ge(oa_out, 2 * PAIRS + FREE)
            pe.wait_ge(ob_out, 2 * PAIRS + FREE)
            pe.wait_ge(mod_ready, 2)
            with pe.Fori(0, 2) as r:
                for s in range(4):
                    b = 4 * (s % 2)
                    pe.wait_ge(ring_in[s], r * 32 + (16 * ADA[s] + 32))
                    pe.wait_ge(merged_ready, r * 4 + max(s - 1, 0) + FREE)
                    wg = ring[:, s, 0:2048].rearrange("p (k n) -> p k n", k=DC)
                    wu = ring[:, s, 2048:3072].rearrange("p (k n) -> p k n", k=2 * PAIRS)
                    for c in range(2):
                        for k in range(DC):
                            last = pe.matmul(ps[b + c][:], wg[:, k, c * P:(c + 1) * P], h[:, k, :], start=(k == 0), stop=(k == DC - 1))
                        last.then_inc(gate_done, 1)
                    for c, y in enumerate((yA, yB)):
                        for k in range(PAIRS):
                            last = pe.matmul(ps[b + 2 + c][:], wu[:, c * PAIRS + k, :], y[:, k, :], start=(k == 0), stop=(k == PAIRS - 1))
                    last.then_inc(up_done, 1)
            pe.wait_ge(merged_ready, DC + FREE)
            for m in range(DC):
                if m % 4 == 0:
                    pe.wait_ge(ring_in[m // 4], 16 * ADA[m // 4] + 32 * 2 + 16)
                if m >= 2:
                    pe.wait_ge(x_ready, m - 1)
                w = ring[:, m // 4, (m % 4) * 1024:(m % 4 + 1) * 1024].rearrange("p (k n) -> p k n", k=DC)
                for k in range(DC):
                    last = pe.matmul(ps[m % 2][:], w[:, k, :], merged[:, k, :], start=(k == 0), stop=(k == DC - 1))
                last.then_inc(out_done, 1)
            rms_sum(DC, squares2)
            pe.wait_ge(h_ready, 2 * DC)
            pe.wait_ge(sk_in, 16)
            with pe.Fori(0, HEADS // 2) as r:
                for s in range(2):
                    pe.wait_ge(ring_in[2 + s], r * 16 + (16 * ADA[2 + s] + 32 * 2 + 16))
                    pe.wait_ge(qry_ready, r * 4 + s * 2 + FREE)
                    w = ring[:, 2 + s, 0:2048].rearrange("p (k n) -> p k n", k=DC)
                    for c in range(2):
                        for k in range(DC):
                            last = pe.matmul(ps[c][:], w[:, k, c * P:(c + 1) * P], h[:, k, :], start=(k == 0), stop=(k == DC - 1))
                        last.then_inc(qry_done, 1)
                    pe.wait_ge(qry_ready, r * 4 + (s * 2 + 2) + FREE)
                    pe.wait_ge(score_ready, r * 4 + s * 2 + FREE)
                    for c in range(2):
                        for t in range(TT):
                            last = pe.matmul(ps[2 + c][:, t * P:(t + 1) * P], qv[:, c, t * P:(t + 1) * P],
                                             skt[:, bass.ds(r * 4 + (s * 2 + c), 1), :].rearrange("p a n -> p (a n)"), start=True, stop=True)
                        last.then_inc(score_done, 1)
                    pe.wait_ge(e_in[s], r * 16 + 16)
                    pe.wait_ge(gelu_ready, r * 2 + FREE)
                    for k in range(DC):
                        last = pe.matmul(ps[4 + s][:], ute[:, s, k * P:(k + 1) * P], h[:, k, :], start=(k == 0), stop=(k == DC - 1))
                    last.then_inc(s_done, 1)
            pe.wait_ge(slots_ready, 3 * HEADS)
            pe.wait_ge(score_ready, 2 * HEADS + FREE)
            for f in range(3):
                for t in range(TT):
                    last = pe.transpose(ps[f][:, t * P:(t + 1) * P], slots[:, f, t, :], ident)
                last.then_inc(slotsT_done, 1)
            pe.wait_ge(slotsT_ready, 3)
            PASSES = ((0, 0), (1, 0), (0, 1))

            def scores(r, e):
                pe.wait_ge(u_split, r * RING + (e + 1))
                pe.wait_ge(gelu_ready, r * RING + (EARLY + e - 1) + FREE)
                for k in range(DC):
                    for q, (wp, xp) in enumerate(PASSES):
                        last = pe.matmul(ps[e % 2][:], us[:, e % 2, wp, k * P:(k + 1) * P], hs[:, xp, k, :],
                                         start=(k == 0 and q == 0), stop=(k == DC - 1 and q == 2))
                last.then_inc(s_done, 1)

            pe.wait_ge(h_split, DC)
            with pe.Fori(0, WITH_G // RING) as r:
                for e in range(RING):
                    scores(r, e)
                    for b in range(2):
                        pe.wait_ge(hot_ready[b], r * 32 + (8 * e + 8))
                        pe.wait_ge(staged[b], r * 4 + e + FREE)
                        for q in range(4):
                            last = pe.matmul(ps[2 + b][:, q * P:(q + 1) * P], ohj[:, b, q, :], ohi[:, b, q, :], start=True, stop=True)
                        last.then_inc(hot_done[b], 1)
            with pe.Fori(WITH_G // RING, (NK - EARLY) // RING) as r:
                for e in range(RING):
                    scores(r, e)

            def values(r, e, first=False):
                pe.wait_ge(v_split, r * RING + (e + 1))
                pe.wait_ge(a_split, r * RING + (e + 1))
                for k in range(DC):
                    for q, (wp, xp) in enumerate(PASSES):
                        last = pe.matmul(ps[k][:], vs[:, e % 2, wp, k * P:(k + 1) * P], ar[:, e % 2, xp, :],
                                         start=(first and q == 0), stop=True, skip_group_check=True)
                last.then_inc(v_done, 1)

            pe.wait_ge(gelu_ready, NK + FREE)
            for e in range(RING):
                values(0, e, first=(e == 0))
            with pe.Fori(1, NK // RING) as r:
                for e in range(RING):
                    values(r, e)
            rms_sum(2 * DC, squares3)

        @block.scalar
        def _(sa):
            start(sa, at_ready, qry_ready, score_ready, gelu_ready, *staged, *e_out, *gelu_out)
            act_ = nc.scalar.activation

            def squares(first, dst):
                for k in range(DC):
                    if k >= 2:
                        sa.wait_ge(sq_summed, first + k - 1)
                    act_(dst[:, k % 2, :], x[:, k, :], ACT.Square).then_inc(sq_ready, 1)

            def root(n):
                sa.wait_ge(var_ready, n)
                act_(rstd[:], var[:], ACT.Sqrt).then_inc(root_ready, 1)

            def modulate(n, mul, shift):
                for k in range(DC):
                    sa.wait_ge(norm_part, n * DC + k + 1)
                    act_(h[:, k, :], h[:, k, :], ACT.Identity, scale=mul[:, k:k + 1], bias=part(shift, k)).then_inc(h_ready, 1)

            sa.wait_ge(smalls_in, 48)
            act_(cact[:], sml[:, S_C:S_C + DC], ACT.Silu).then_inc(cact_ready, 1)
            sa.wait_ge(angle_ready, 2)
            act_(sinT, sinT, ACT.Sin).then_inc(trig_ready, 1)
            act_(cosT, cosT, ACT.Sin).then_inc(trig_ready, 1)
            sa.wait_ge(x_in, 16)
            squares(0, spl)
            root(1)
            sa.wait_ge(mod_ready, 1)
            modulate(0, mul1, 0)
            sa.wait_ge(proj_done, 1)
            act_(qraw, ps[0][:], ACT.Copy).then_inc(q_raw_ready, 1)
            sa.wait_ge(va_done, 1)
            act_(vA.rearrange("p a b -> p (a b)"), ps[1][:], ACT.Copy).then_inc(va_ready, 1)
            sa.wait_ge(rope_ready, 1)

            with sa.Fori(0, PAIRS) as i:
                sa.wait_ge(proj_done, i * 4 + 2)
                act_(qraw, ps[0][:], ACT.Copy, scale=HD ** -0.5).then_inc(q_raw_ready, 1)
                for c, dst in ((1, qB), (2, kB), (3, vB.rearrange("p a b -> p (a b)"))):
                    sa.wait_ge(proj_done, i * 4 + (2 + c))
                    act_(dst, ps[c][:], ACT.Copy, scale=HD ** -0.5 if c == 1 else 1.0).then_inc(evac_done, 1)
                for a in range(2):
                    for b in range(4):
                        sa.wait_ge(sb_scored, i * 8 + (a * 4 + b + 1))
                        act_(spl[:, b, b * P:T], ps[4 + b][:, b * P:T], ACT.Abs).then_inc(abs_ready, 1)
                    for b in range(4):
                        sa.wait_ge(abs_ready, i * 8 + (a * 4 + b + 1))
                        act_(spl[:, b, b * P:T], spl[:, b, b * P:T], ACT.Exp, scale=-1.0).then_inc(act_steps, 1)
                    sa.wait_ge(max_ready, i * 2 + (a + 1))
                    for t in range(TT):
                        act_(prob[:, t, :], ps[t // 2][:, (t % 2) * 256:(t % 2) * 256 + 256], ACT.Exp,
                             bias=mx[:, 4 + t:5 + t], accum_out=sk4[:, t:t + 1]).then_inc(swa_exp, 1)
                    act_(sk4[:, 4:8], mx[:, 4:8], ACT.Exp, bias=sml[:, bass.ds(i * 2 + (S_SINK + a), 1)]).then_inc(swa_exp, 1)
                    for b in range(4):
                        sa.wait_ge(act_steps, i * 8 + (a * 4 + b + 1))
                        act_(spl[:, b, b * P:T], spl[:, b, b * P:T], ACT.Ln, bias=1.0).then_inc(log_ready, 1)
                    sa.wait_ge(probT_done, i * 2 + (a + 1))
                    for c in range(2):
                        last = act_(probT[:, 2 * c:2 * c + 2, :].rearrange("p a b -> p (a b)"), ps[2 + c][:], ACT.Copy)
                    last.then_inc(probT_ready, 1)
                    for b in range(4):
                        sa.wait_ge(sb_summed, i * 8 + (a * 4 + b + 1))
                        act_(atB[:, b, b * P:T], ps[4 + b][:, b * P:T], ACT.Exp).then_inc(at_ready, 1)

            with sa.Fori(0, DC // 2) as r:
                for s in range(2):
                    sa.wait_ge(merged_ready, r * 2 + FREE)
                    for c, dst in enumerate((siga, sigb)):
                        sa.wait_ge(gate_done, r * 4 + (s * 2 + c + 1))
                        act_(dst[:, s, :], ps[4 * s + c][:], ACT.Sigmoid).then_inc(sig_ready, 1)
            sa.wait_ge(x_ready, DC)
            squares(DC, squares2)
            root(2)
            sa.wait_ge(mod_ready, 2)
            modulate(1, mul2, 3)
            for k in range(DC):
                sa.wait_ge(h_ready, DC + k + 1)
                act_(hs[:, 0, k, :], h[:, k, :], ACT.Copy).then_inc(hi_ready, 1)
            with sa.Fori(0, HEADS // 2) as r:
                for s in range(2):
                    sa.wait_ge(score_done, r * 4 + 2 * s + FREE)
                    for c in range(2):
                        sa.wait_ge(qry_done, r * 4 + (2 * s + c + 1) + FREE)
                        act_(qv[:, c, :], ps[c][:], ACT.Copy).then_inc(qry_ready, 1)
                    sa.wait_ge(score_used, r * 2 + s + FREE)
                    for c in range(2):
                        sa.wait_ge(score_done, r * 4 + (2 * s + c + 1) + FREE)
                        act_(sc[:, c, :, :].rearrange("p a b -> p (a b)"), ps[2 + c][:], ACT.Copy).then_inc(score_ready, 1)
                    sa.wait_ge(s_done, r * 2 + (s + 1) + FREE)
                    sa.wait_ge(e_out[s], r * 16 + FREE)
                    act_(gele[:, s, :], ps[4 + s][:], ACT.Gelu).then_inc(gelu_ready, 1)
                    sa.wait_ge(gelu_ready, r * 2 + (s + 1) + FREE)
                    sa.dma_start(row(gelu_dram, r * 2 + s), gele[:, s, :]).then_inc(e_out[s], 16)
                    sa.wait_ge(best_ready, r * 2 + (s + 1))
                    act_(bv.rearrange("p a b -> p (a b)"), bv.rearrange("p a b -> p (a b)"), ACT.Exp).then_inc(best_exp, 1)
            for f in range(3):
                sa.wait_ge(slotsT_done, f + 1)
                act_(slotsT[:, f, :], ps[f][:], ACT.Copy).then_inc(slotsT_ready, 1)
            def u_high(r, e):
                sa.wait_ge(u_in[e], r * 16 + 16)
                act_(us[:, e % 2, 0, :], ut[:, e, :], ACT.Copy).then_inc(u_hi, 1)

            def gelus(r, e, ahead=True):
                sa.wait_ge(s_done, r * RING + (EARLY + e + 1) + FREE)
                sa.wait_ge(gelu_out[e], r * 16 + FREE)
                act_(gel[:, e, :], ps[e % 2][:], ACT.Gelu).then_inc(gelu_ready, 1)
                if ahead:
                    u_high(r + (e + 2) // RING, (e + 2) % RING)
                sa.wait_ge(gelu_ready, r * RING + (EARLY + e + 1) + FREE)
                sa.dma_start(row(gelu_dram, r * RING + (EARLY + e)), gel[:, e, :]).then_inc(gelu_out[e], 16)

            for c in range(2):
                sa.wait_ge(e_out[c], 16 * EARLY // 2 + FREE)
            u_high(0, 0)
            u_high(0, 1)
            with sa.Fori(0, T // 128) as q:
                for c in range(2):
                    sa.wait_ge(stage_free[c], q + FREE)
                    with sa.Fori(0, 2) as r:
                        for e in range(RING):
                            gelus(q * 4 + r + 2 * c, e)
                            for b in range(2):
                                sa.wait_ge(hot_done[b], q * 16 + r * 4 + (8 * c + e + 1) + FREE)
                                act_(stages[c][:, :, bass.ds(r * 32 + (e * 8 + b * 4), 4)],
                                     ps[2 + b][:].rearrange("p (t i) -> p i t", t=4), ACT.Copy).then_inc(staged[b], 1)
            with sa.Fori(WITH_G // RING, last_turn) as r:
                for e in range(RING):
                    gelus(r, e)
            for e in range(RING):
                gelus(last_turn, e, ahead=(e < 2))
            def v_high(r, e):
                sa.wait_ge(v_in[e], r * 16 + 16)
                if not isinstance(r, int) or e >= 2:
                    sa.wait_ge(v_done, r * RING + (e - 1) + FREE)
                act_(vs[:, e % 2, 0, :], vt[:, e, :], ACT.Copy).then_inc(v_hi, 1)

            for e in range(RING):
                v_high(0, e)
            with sa.Fori(1, NK // RING) as r:
                for e in range(RING):
                    v_high(r, e)
            sa.wait_ge(x_ready, 2 * DC)
            squares(2 * DC, squares3)
            root(3)

        @block.vector
        def _(ve):
            start(ve, *ring_free, oa_out, ob_out, merged_ready, score_used)
            nv = nc.vector
            step = Steps(ve, dve_steps)
            step.pad = pad[:]

            def inv_rms(n):
                ve.wait_ge(sq_summed, n * DC)
                nv.tensor_scalar(var[:], ps[7][:], 1.0 / D, EPS, ALU.mult, ALU.add).then_inc(var_ready, 1)
                ve.wait_ge(root_ready, n)
                step(nv.reciprocal(rstd[:], rstd[:]))

            def ada_product(n, slot, b, loads):
                ve.wait_ge(ring_in[slot], loads * 16)
                if not isinstance(n, int) or n >= 2:
                    ve.wait_ge(ada_summed, n - 1)
                w = ring[:, slot, :].rearrange("p (k n) -> p k n", k=DC)
                step(nv.tensor_scalar(adap[:, b, :], w[:, 0, :], cact[:, 0:1], None, ALU.mult))
                for k in range(1, DC):
                    ins = nv.scalar_tensor_tensor(adap[:, b, :], w[:, k, :], cact[:, k:k + 1], adap[:, b, :], ALU.mult, ALU.add)
                    if k < DC - 1:
                        step(ins)
                ins.then_inc(ada_ready, 1)
                ve.wait_ge(ada_ready, n + 1)
                ve.sem_inc(ring_free[slot], 1)

            ve.wait_ge(smalls_in, 48)
            step(nv.tensor_copy(turn, ang.bitcast(I32)))
            step(nv.tensor_scalar(ang, turn, cst[:, K_INV:K_INV + 1], None, ALU.mult))
            for dst, quarter in ((sinT, 0.0), (cosT, 0.25)):
                step(nv.tensor_scalar(turn, ang, 1 / TWO_PI, quarter, ALU.mult, ALU.add))
                step(nv.tensor_scalar(turn, turn, MAGIC, None, ALU.add))
                step(nv.tensor_scalar(turn, turn, -MAGIC, None, ALU.add))
                step(nv.scalar_tensor_tensor(dst, turn, -C1, ang, ALU.mult, ALU.add))
                step(nv.scalar_tensor_tensor(dst, turn, -C2, dst, ALU.mult, ALU.add))
                step(nv.scalar_tensor_tensor(dst, turn, -C3, dst, ALU.mult, ALU.add))
                step(nv.tensor_scalar(dst, dst, quarter * TWO_PI, None, ALU.add))
                nv.tensor_scalar(dst, dst, -3.1415925, 3.1415925, ALU.max, ALU.min).then_inc(angle_ready, 1)
            inv_rms(1)
            for k in range(DC):
                ve.wait_ge(x_in, 16)
                nv.tensor_tensor(h[:, k, :], x[:, k, :], rstd[:], ALU.mult).then_inc(norm_part, 1)
            ve.wait_ge(cact_ready, 1)
            for n in range(4):
                ada_product(n, n, n % 2, 1)
            ve.wait_ge(ada_summed, 4)
            step(nv.tensor_tensor(mod[:, 0:16], ps[6][:, 0:16], sml[:, S_B:S_B + 16], ALU.add))
            nv.scalar_tensor_tensor(mul1[:], part(1), 1.0, sml[:, S_G1:S_G1 + DC], ALU.add, ALU.mult).then_inc(mod_ready, 1)

            def rope(n, dst):
                ve.wait_ge(q_raw_ready, n)
                step(nv.tensor_tensor(dst, qraw, cosT, ALU.mult))
                ve.wait_ge(rot_done, n)
                step(nv.tensor_tensor(ang, ps[4][:], sinT, ALU.mult))
                nv.tensor_tensor(dst, dst, ang, ALU.add).then_inc(rope_ready, 1)

            ve.wait_ge(trig_ready, 2)
            rope(1, kR)

            with ve.Fori(0, PAIRS) as i:
                step.enter(i, 24)
                for a in range(2):
                    ada_product(i * 2 + (4 + a), a, a, i + 2)
                rope(i + 2, qR)
                for a in range(2):
                    lo, hi = a * HD, (a + 1) * HD
                    ve.wait_ge(swa_scored, i * 2 + (a + 1))
                    for c in range(2):
                        ins = nv.tensor_reduce(mx[:, 2 * c:2 * c + 2], ps[c][:].rearrange("p (a b) -> p a b", a=2), AX.X, ALU.max)
                    step(ins)
                    nv.tensor_scalar(mx[:, 4:8], mx[:, 0:4], sml[:, bass.ds(i * 2 + (S_SINK + a), 1)], -1.0,
                                     ALU.max, ALU.mult).then_inc(max_ready, 1)
                    ve.wait_ge(swa_exp, i * 10 + (a * 5 + 5))
                    step(nv.tensor_tensor(sk4[:, 8:12], sk4[:, 0:4], sk4[:, 4:8], ALU.add))
                    step(nv.reciprocal(sk4[:, 12:16], sk4[:, 8:12]))
                    for t in range(TT):
                        ins = nv.tensor_scalar(prob[:, t, :], prob[:, t, :], sk4[:, 12 + t:13 + t], None, ALU.mult)
                    ins.then_inc(prob_ready, 1)
                    for b in range(4):
                        ve.wait_ge(log_ready, i * 8 + (a * 4 + b + 1))
                        ins = nv.scalar_tensor_tensor(spl[:, b, b * P:T], ps[4 + b][:, b * P:T], 0.0, spl[:, b, b * P:T],
                                                      ALU.max, ALU.add)
                    step(ins)
                    for b in range(4):
                        nv.tensor_tensor(spl[:, b, b * P:(b + 1) * P], spl[:, b, b * P:(b + 1) * P], cst[:, K_CAUS:K_CAUS + P],
                                         ALU.mult).then_inc(sp_ready, 1)
                    ve.wait_ge(oa_done, i * 2 + (a + 1))
                    nv.tensor_copy(yA[lo:hi, bass.ds(i, 1), :].rearrange("p a n -> p (a n)"), ps[0][lo:hi, :]).then_inc(oa_out, 1)
                    ve.wait_ge(ob_done, i * 2 + (a + 1))
                    nv.tensor_copy(yB[lo:hi, bass.ds(i, 1), :].rearrange("p a n -> p (a n)"), ps[1][lo:hi, :]).then_inc(ob_out, 1)
                step.leave(PAIRS)

            ve.wait_ge(ada_summed, 12)
            step(nv.tensor_tensor(mod[:, 16:48], ps[7][:, 0:32], sml[:, S_B + 16:S_B + 48], ALU.add))
            nv.scalar_tensor_tensor(mul2[:], part(4), 1.0, sml[:, S_G2:S_G2 + DC], ALU.add, ALU.mult).then_inc(mod_ready, 1)
            with ve.Fori(0, DC // 2) as r:
                step.enter(r, 2)
                for s in range(2):
                    ve.wait_ge(sig_ready, r * 4 + (s * 2 + 2))
                    ve.wait_ge(up_done, r * 2 + (s + 1))
                    nv.tensor_tensor(ma[:, s, :], siga[:, s, :], ps[4 * s + 2][:], ALU.mult)
                    step(nv.tensor_tensor(mb[:, s, :], sigb[:, s, :], ps[4 * s + 3][:], ALU.mult))
                    nv.tensor_tensor(merged[:, bass.ds(r * 2 + s, 1), :].rearrange("p a n -> p (a n)"),
                                     ma[:, s, :], mb[:, s, :], ALU.add).then_inc(merged_ready, 1)
                step.leave(DC // 2)
            for m in range(DC):
                ve.wait_ge(out_done, m + 1)
                nv.scalar_tensor_tensor(x[:, m, :], ps[m % 2][:], part(2, m), x[:, m, :], ALU.mult, ALU.add).then_inc(x_ready, 1)
            inv_rms(2)
            for k in range(DC):
                nv.tensor_tensor(h[:, k, :], x[:, k, :], rstd[:], ALU.mult).then_inc(norm_part, 1)

            for k in range(DC):
                ve.wait_ge(hi_ready, k + 1)
                nv.tensor_tensor(hs[:, 1, k, :], h[:, k, :], hs[:, 0, k, :].bitcast(F32), ALU.subtract).then_inc(h_split, 1)

            with ve.Fori(0, HEADS) as i:
                step.enter(i, 13)
                step.wait_apart(score_ready, i * 2 + 2 + FREE)
                every = [(c, t) for c in range(2) for t in range(TT)]

                for c, t in every:
                    ins = nv.max(tv[:, c, t, 0:8], sc[:, c, t, :])
                step(ins, apart=True)
                for c, t in every:
                    nv.max_index(ti[:, c, t, 0:8], tv[:, c, t, 0:8], sc[:, c, t, :])
                    ins = nv.match_replace(sc2[:, c, t, :], tv[:, c, t, 0:8], sc[:, c, t, :], LOWEST)
                ins.then_inc(score_used, 1)
                step.wait_apart(score_used, i + 1 + FREE)
                for c, t in every:
                    ins = nv.max(tv[:, c, t, 8:16], sc2[:, c, t, :])
                step(ins, apart=True)
                for c, t in every:
                    nv.max_index(ti[:, c, t, 8:16], tv[:, c, t, 8:16], sc2[:, c, t, :])
                for t in range(TT):
                    ins = nv.tensor_tensor(cand[:, t, :].rearrange("p (a b) -> p a b", a=TOPK),
                                           tv[:, 0, t, :].unsqueeze(2).to_broadcast([P, TOPK, TOPK]),
                                           tv[:, 1, t, :].unsqueeze(1).to_broadcast([P, TOPK, TOPK]), ALU.add)
                step(ins, apart=True)
                for t in range(TT):
                    ins = nv.max(bv[:, t, 0:8], cand[:, t, :])
                step(ins, apart=True)
                for t in range(TT):
                    nv.max_index(bi[:, t, 0:8], bv[:, t, 0:8], cand[:, t, :])
                    ins = nv.match_replace(cand2[:, t, :], bv[:, t, 0:8], cand[:, t, :], LOWEST)
                step(ins, apart=True)
                for t in range(TT):
                    ins = nv.max(bv[:, t, 8:16], cand2[:, t, :])
                step(ins, apart=True)
                for t in range(TT):
                    ins = nv.max_index(bi[:, t, 8:16], bv[:, t, 8:16], cand2[:, t, :])
                nv.tensor_copy(den[:, 0:TT], bv[:, :, 0:1].rearrange("p a b -> p (a b)"))
                step(nv.tensor_copy(tif.rearrange("p a b c -> p (a b c)"), ti.rearrange("p a b c -> p (a b c)")))
                nv.tensor_tensor(bv, bv, den[:, 0:TT].unsqueeze(2).to_broadcast([P, TT, TOPK]), ALU.subtract).then_inc(best_ready, 1)
                bif = bi.rearrange("p a b -> p (a b)")
                nv.tensor_scalar(bij[:, 0, :], bif, 4, None, ALU.logical_shift_right)
                step(nv.tensor_scalar(bij[:, 1, :], bif, 15, None, ALU.bitwise_and))
                step(nv.tensor_copy(bijf.rearrange("p a b -> p (a b)"), bij.rearrange("p a b -> p (a b)")))
                for c in range(2):
                    ins = nv.tensor_tensor(pick[:, c, :, :], bijf[:, c, :].unsqueeze(2).to_broadcast([P, TT * TOPK, TOPK]),
                                           cst[:, K_IOTA:K_IOTA + TOPK].unsqueeze(1).to_broadcast([P, TT * TOPK, TOPK]), ALU.is_equal)
                step(ins)
                for c in range(2):
                    p4 = pick[:, c, :, :].rearrange("p (t s) k -> p t s k", t=TT)
                    ins = nv.tensor_tensor(p4, p4, tif[:, c, :, :].unsqueeze(2).to_broadcast([P, TT, TOPK, TOPK]), ALU.mult)
                step(ins)
                for c in range(2):
                    nv.tensor_reduce(slots[:, c, :, bass.ds(i * TOPK, TOPK)], pick[:, c, :, :].rearrange("p (t s) k -> p t s k", t=TT),
                                     AX.X, ALU.add).then_inc(slots_ready, 1)
                ve.wait_ge(best_exp, i + 1)
                step(nv.tensor_reduce(den[:, 0:TT], bv, AX.X, ALU.add))
                step(nv.reciprocal(den[:, TT:2 * TT], den[:, 0:TT]))
                nv.tensor_tensor(slots[:, 2, :, bass.ds(i * TOPK, TOPK)], bv, den[:, TT:2 * TT].unsqueeze(2).to_broadcast([P, TT, TOPK]),
                                 ALU.mult).then_inc(slots_ready, 1)
                step.leave(HEADS)

            ve.wait_ge(slotsT_ready, 3)

            def u_low(r, e):
                ve.wait_ge(u_hi, r * RING + (e + 1))
                nv.tensor_tensor(us[:, e % 2, 1, :], ut[:, e, :], us[:, e % 2, 0, :].bitcast(F32), ALU.subtract).then_inc(u_split, 1)

            u_low(0, 0)
            u_low(0, 1)
            with ve.Fori(0, WITH_G // RING) as r:
                for e in range(RING):
                    for b in range(2):
                        ve.wait_ge(hot_done[b], r * 4 + e + FREE)
                        for q in range(4):
                            def col(f):
                                return slotsT[:, f, bass.ds(r * 32 + (e * 8 + b * 4 + q), 1)]
                            nv.tensor_scalar(ohi[:, b, q, :], cst[:, K_IOTA:K_IOTA + P], col(0), None, ALU.is_equal).then_inc(hot_ready[b], 1)
                            nv.tensor_scalar(ohj[:, b, q, :], cst[:, K_IOTA:K_IOTA + P], col(1), col(2), ALU.is_equal,
                                             ALU.mult).then_inc(hot_ready[b], 1)
                    u_low(r + (e + 2) // RING, (e + 2) % RING)
            with ve.Fori(WITH_G // RING, last_turn) as r:
                for e in range(RING):
                    u_low(r + (e + 2) // RING, (e + 2) % RING)
            for e in range(2):
                u_low(last_turn, e + 2)

            def weigh(r, e):
                b = e % 2
                ve.wait_ge(g_in[e], r * 32 + 32)
                nv.tensor_tensor(wgt[:, b, :], gl[:, e, :], gt[:, e, :], ALU.mult).then_inc(w_ready, 1)
                ve.wait_ge(v_hi, r * RING + (e + 1))
                nv.tensor_tensor(vs[:, b, 1, :], vt[:, e, :], vs[:, b, 0, :].bitcast(F32), ALU.subtract).then_inc(v_split, 1)
                ve.wait_ge(w_ready, r * RING + (e + 1))
                nv.tensor_copy(ar[:, b, 0, :], wgt[:, b, :]).then_inc(a_hi, 1)
                ve.wait_ge(a_hi, r * RING + (e + 1))
                nv.tensor_tensor(ar[:, b, 1, :], wgt[:, b, :], ar[:, b, 0, :].bitcast(F32), ALU.subtract).then_inc(a_split, 1)

            for e in range(RING):
                weigh(0, e)
            with ve.Fori(1, NK // RING) as r:
                for e in range(RING):
                    weigh(r, e)
            ve.wait_ge(v_done, NK + FREE)
            for k in range(DC):
                nv.scalar_tensor_tensor(x[:, k, :], ps[k][:], part(5, k), x[:, k, :], ALU.mult, ALU.add).then_inc(x_ready, 1)
            inv_rms(3)
            ve.wait_ge(x_ready, 2 * DC)
            for k in range(DC):
                nv.scalar_tensor_tensor(h[:, k, :], x[:, k, :], sml[:, S_GF + k:S_GF + k + 1], rstd[:], ALU.mult, ALU.mult).then_inc(y_ready, 1)


def constants():
    k = np.zeros((P, K_END), np.float32)
    p, f = np.arange(P)[:, None], np.arange(P)[None, :]
    k[:, K_ID:K_ID + P] = p == f
    k[:, K_ONE:K_ONE + P] = 1.0
    k[:, K_NTRI:K_NTRI + P] = np.where(p >= f, -1.0, 0.0)
    k[:, K_NONE:K_NONE + P] = -1.0
    k[:, K_SBM:K_SBM + P] = np.where(p >= f, BIG, 0.0)
    k[:, K_CAUS:K_CAUS + P] = p < f
    half = HD // 2
    for m in range(P):
        if m % HD < half:
            k[m + half, K_ROT + m] = -1.0
        else:
            k[m - half, K_ROT + m] = 1.0
    k[:, K_IOTA:K_IOTA + P] = f
    q, c = np.arange(P)[:, None] // HD, np.arange(2 * P)[None, :] // HD - 2
    ok = (c == q) | (c == q - 1)
    k[:, K_SWA:K_SWA + 256] = np.where(ok, 0.0, BIG)
    k[:, K_SWA0:K_SWA0 + 256] = np.where(ok & (c >= 0), 0.0, BIG)
    k[:, K_INV] = np.float32(10000.0) ** (-(np.arange(P) % half).astype(np.float32) / np.float32(half))
    return k


def kernel(x, c, positions, norm1_g, norm2_g, final_g, w_ada, b_ada, w_in, sinks,
           w_up_swa, w_up_sb, w_out, w_query, sub_keys, expert_u, expert_v):
    import concourse.bacc as bacc
    from concourse.bass_utils import run_bass_kernel_spmd

    def columns(v):
        return np.asarray(v).reshape(-1, P).T

    def tiles(w):
        w = np.asarray(w)
        return w.reshape(w.shape[0] // P, P, w.shape[1]).transpose(1, 0, 2)

    order = np.array([h * HD + d for i in range(PAIRS) for h in (i, i + PAIRS) for d in range(HD)])
    pair_sinks = np.asarray(sinks)[0][[h for i in range(PAIRS) for h in (i, i + PAIRS)]]
    small = np.concatenate([columns(c[0]), columns(norm1_g[0]), columns(norm2_g[0]), columns(final_g),
                            columns(b_ada[0]), np.repeat(pair_sinks[None], P, 0)], 1)
    wi = np.asarray(w_in)[0]
    qa, kv, qb, kb, vb, g = (wi[:, 0:512][:, order], wi[:, 512:768], wi[:, 768:1280], wi[:, 1280:1792],
                             wi[:, 1792:2304], wi[:, 2304:])
    pair = np.stack([tiles(np.concatenate([w[:, i * P:(i + 1) * P] for w in (qa, qb, kb, vb)], 1)).reshape(P, -1)
                     for i in range(PAIRS)])
    gate = np.stack([tiles(np.concatenate([g[:, m * P:(m + 1) * P], g[:, D + m * P:D + (m + 1) * P]], 1)).reshape(P, -1)
                     for m in range(DC)])
    ups = np.concatenate([np.asarray(w_up_swa)[0][order], np.asarray(w_up_sb)[0]], 0)
    up = np.stack([tiles(ups[:, m * P:(m + 1) * P]).reshape(P, -1) for m in range(DC)])
    wo = np.asarray(w_out)[0]
    out = np.stack([tiles(wo[:, m * P:(m + 1) * P]).reshape(P, -1) for m in range(DC)])
    wq = np.asarray(w_query)[0]
    qry = np.stack([tiles(wq[:, m * 256:(m + 1) * 256]).reshape(P, -1) for m in range(HEADS)])
    wa = np.asarray(w_ada)[0]
    ada = np.stack([tiles(wa[:, m * 512:(m + 1) * 512]).reshape(P, -1) for m in range(12)])
    skT = np.asarray(sub_keys)[0].reshape(2 * HEADS, NK, P).transpose(2, 0, 1)
    eu = np.asarray(expert_u)[0].reshape(NK, P, DC, P).transpose(0, 3, 2, 1).reshape(NK, P, DC * P)
    arrays = {
        "xT": tiles(np.asarray(x)[0].T), "small": small, "consts": constants(), "pos": np.asarray(positions),
        "w_ada": ada, "w_kava": tiles(kv), "w_pair": pair, "w_gate": gate, "w_up": up, "w_out": out, "w_qry": qry,
        "skT": skT, "euT": eu, "ev": np.asarray(expert_v)[0].reshape(NK, P, D),
    }
    nc = bacc.Bacc("TRN2", target_bir_lowering=False, num_devices=1)
    arrays = {k: np.ascontiguousarray(a) for k, a in arrays.items()}
    args = [nc.dram_tensor(k, a.shape, mybir.dt.from_np(a.dtype), kind="ExternalInput").ap() for k, a in arrays.items()]
    args.append(nc.dram_tensor("outT", (P, DC, T), F32, kind="ExternalOutput").ap())
    build(nc, *args)
    got = run_bass_kernel_spmd(nc, [arrays], core_ids=[0]).results[0]["outT"]
    return np.ascontiguousarray(got.transpose(2, 1, 0)).reshape(1, T, D)
```

```python
from contextlib import ExitStack

import numpy as np
import concourse.bass as bass
from concourse import mybir

P = 128
T = 512
D = 1024
TT = T // P
DC = D // P
NMOD = 6
HD = 64
PAIRS = 4
HEADS = 8
TOPK = 16
CAND = 4 * 16 + 12 * 4
NK = 128
RING = 4
EARLY = 12
WITH_G = T // 8
ADA = (5, 5, 1, 1)
SUM_BANKS = (7, 7, 0)
FREE = 1
EPS = 1e-6
BIG = -1e30
LOWEST = -3.0e38
MAGIC = 12582912.0
TWO_PI = 2 * np.pi
C1 = 6.28125
C2 = float(np.float32(1935.0 * 2.0 ** -20))
C3 = float(TWO_PI - C1 - C2)

ALU = mybir.AluOpType
ACT = mybir.ActivationFunctionType
F32 = mybir.dt.float32
F32R = mybir.dt.float32r
U32 = mybir.dt.uint32
I32 = mybir.dt.int32
AX = mybir.AxisListType

(K_ID, K_ONE, K_NTRI, K_NONE, K_SBM, K_CAUS, K_ROT, K_IOTA, K_NEVER, K_SWA, K_INV, K_EPS, K_END) = (
    0, 128, 256, 384, 512, 640, 768, 896, 1024, 1152, 1408, 1409, 1410)
S_C, S_G1, S_G2, S_GF, S_B, S_SINK, S_END = 0, 8, 16, 24, 32, 80, 88

UNITS = ([("up", m, 0) for m in range(4)]
         + [u for m in range(4, DC) for u in (("gate", m, 0), ("gate", m, 1), ("up", m, 0))]
         + [("out", m, 0) for m in range(DC)])
PASSES = ((0, 0), (1, 0), (0, 1))


class Steps:

    def __init__(self, engine, sem):
        self.engine, self.sem, self.n, self.at = engine, sem, 0, 0

    def __call__(self, instruction, apart=False):
        instruction.then_inc(self.sem, 1)
        self.n += 1
        if apart:
            self.wait_apart(self.sem, self.at + self.n)
        else:
            self.engine.wait_ge(self.sem, self.at + self.n)

    def wait_apart(self, sem, value):
        self.engine.wait_ge(sem, value)
        self.engine.memset(self.pad, 0.0)

    def enter(self, i, per_turn):
        self.before, self.per = self.n, per_turn
        self.at, self.n = i * per_turn + self.before, 0

    def leave(self, turns):
        assert self.n == self.per, (self.n, self.per)
        self.at, self.n = 0, self.before + turns * self.per


def row(a, i):
    return a[bass.ds(i, 1), :, :].rearrange("a p n -> p (a n)")


def build(nc, xT, small, consts, pos, w_ada, w_kava, w_pair, w_gate, w_units, w_qry, skT, euT, ev, outT):
    with ExitStack() as ctx:
        def sb(name, shape, dt=F32):
            return ctx.enter_context(nc.sbuf_tensor(name, shape, dt))

        def sem(name):
            return ctx.enter_context(nc.semaphore(name))

        ps = [ctx.enter_context(nc.psum_tensor(f"bank{n}", [P, 512], F32)) for n in range(8)]
        gelu_dram = nc.dram_tensor("gelu_scratch", (NK, P, T), F32, kind="Internal").ap()
        gates_dram = nc.dram_tensor("gates_scratch", (NK, P, T), F32, kind="Internal").ap()

        cst = sb("cst", [P, K_END])
        sml = sb("sml", [P, S_END])
        x = sb("x", [P, DC, T])
        h = sb("h", [P, DC, T])
        mod = sb("mod", [P, NMOD * DC])
        mul1 = sb("mul1", [P, DC])
        mul2 = sb("mul2", [P, DC])
        cact = sb("cact", [P, DC])
        rstd = sb("rstd", [P, T])
        pad = sb("pad", [P, 1])
        tiny = sb("tiny", [P, 1])
        ident = cst[:, K_ID:K_ID + P]
        ones = cst[:, K_ONE:K_ONE + P]

        def part(m, k=None):
            return mod[:, m * DC:(m + 1) * DC] if k is None else mod[:, m * DC + k:m * DC + k + 1]

        ARENA = 164 * 256
        arena_at = -(-nc.sbuf_base // 64) * 64
        arena = nc.alloc_sbuf_tensor_at("arena", [P, ARENA], F32, offset=arena_at)
        top = [0]

        def carve(*shape, split=None):
            n = int(np.prod(shape))
            if split:
                a = nc.alloc_sbuf_tensor_at(split, [P, n], F32R, offset=arena_at + 4 * top[0])[:]
            else:
                a = arena[:, top[0]:top[0] + n]
            top[0] += n
            assert top[0] <= ARENA, top[0]
            if len(shape) == 2:
                a = a.rearrange("p (a b) -> p a b", a=shape[0])
            if len(shape) == 3:
                a = a.rearrange("p (a b c) -> p a b c", a=shape[0], b=shape[1])
            return a

        ring = carve(4, 4096)
        front = top[0]
        pairw = carve(DC, 512)
        cosT = carve(T)
        sinT = carve(T)
        ang = carve(T)
        turn = carve(T)
        kR = carve(T)
        vA = carve(TT, P)
        qraw = carve(T)
        qR = carve(T)
        qB = carve(T)
        kB = carve(T)
        vB = carve(TT, P)
        prob = carve(TT, 256)
        probT = carve(TT, 256)
        spl = carve(4, T)
        atB = carve(4, T)
        kavaw = atB.rearrange("p a n -> p (a n)").rearrange("p (k n) -> p k n", k=DC)
        adap = carve(2, T)
        mx = carve(8)
        sk4 = carve(16)
        early_gates = carve(DC, T)
        att_end = top[0]
        top[0] = front - 1024
        ident_r = carve(P, split="ident_r")
        window_r = carve(256, split="window_r")
        never_r = carve(P, split="never_r")
        after_r = carve(P, split="after_r")
        assert top[0] <= front
        top[0] = 0
        wraw = carve(4, D)
        top[0] = 8192
        siga = carve(2, T)
        sigb = carve(2, T)
        ma = carve(2, T)
        mb = carve(2, T)
        ws = carve(2, 2, D, split="unit_split")
        assert top[0] == front
        h1s = carve(2 * DC, T, split="h1_split").rearrange("p (s k) n -> p s k n", s=2)
        ys = carve(2 * DC, T, split="y_split").rearrange("p (s k) n -> p s k n", s=2)
        assert top[0] <= att_end - DC * T
        merged = h
        ms = h1s
        y8 = arena[:, ARENA - 2 * PAIRS * T:ARENA].rearrange("p (a b) -> p a b", a=2 * PAIRS)
        yA = y8[:, 0:PAIRS, :]
        yB = y8[:, PAIRS:, :]
        assert att_end <= ARENA - 2 * PAIRS * T, att_end
        squares2 = yB[:, 2:4, :]
        top[0] = 0
        stages = (carve(NK, 64), carve(NK, 64))
        ohi = carve(2, 4, P)
        ohj = carve(2, 4, P)
        slotsT = carve(3, T)
        top_k_at = top[0]
        skt = carve(2 * HEADS, P)
        qv = carve(2, T)
        sc = carve(2, TT, P)
        sc2 = carve(2, TT, P)
        tv = carve(2, TT, TOPK)
        ti = carve(2, TT, TOPK).bitcast(U32)
        tif = carve(2, TT, TOPK)
        cand = carve(TT, CAND)
        cand2 = carve(TT, CAND)
        bv = carve(TT, TOPK)
        bi = carve(TT, TOPK).bitcast(U32)
        shifted = carve(2, TT * TOPK).bitcast(U32)
        shiftedf = carve(3, TT * TOPK)
        edge = carve(2, TT * TOPK)
        bijf = carve(2, TT * TOPK)
        pick = carve(2, TT * TOPK, TOPK)
        den = carve(2 * TT)
        slots = carve(3, TT, P)
        top_k_end = top[0]
        top[0] = 0
        ute = carve(2, DC * P)
        gele = carve(2, T)
        assert top[0] <= 2 * 4096
        top[0] = top_k_at
        ut = carve(RING, DC * P)
        us = carve(2, 2, DC * P, split="u_split")
        gel = carve(RING, T)
        top[0] = max(top[0], top_k_end)
        hs = carve(2 * DC, T, split="h_split").rearrange("p (s k) n -> p s k n", s=2)
        q_parts = [[nc.alloc_sbuf_tensor_at(f"query_{half}{s}", [P, 2048], F32R, offset=arena_at + 4 * at)[:]
                    for half, at in (("hi", ats[0]), ("lo", ats[1]))] for s, ats in enumerate(((4096, 6144), (10240, 14336)))]
        top[0] = 0
        vt = carve(RING, D)
        vs = carve(2, 2, D, split="v_split")
        gl = carve(RING, T)
        gt = carve(RING, T)
        wgt = carve(2, T)
        ar = carve(2, 2, T, split="a_split")
        assert top[0] <= top_k_at
        squares3 = wgt

        smalls_in, x_in, kava_in, pair_in, sk_in = map(sem, ("smalls_in", "x_in", "kava_in", "pair_in", "sk_in"))
        ring_in = [sem(f"ring_in{s}") for s in range(4)]
        ring_free = [sem(f"ring_free{s}") for s in range(4)]
        ada_ready, ada_summed, ada_direct = sem("ada_ready"), sem("ada_summed"), sem("ada_direct")
        hi_ready, h_split, u_hi, u_split, v_hi, v_split, a_split = map(sem, (
            "hi_ready", "h_split", "u_hi", "u_split", "v_hi", "v_split", "a_split"))
        cact_ready, mod_ready = sem("cact_ready"), sem("mod_ready")
        sq_ready, sq_summed, root_ready, norm_part, h_ready = map(sem, (
            "sq_ready", "sq_summed", "root_ready", "norm_part", "h_ready"))
        dve_steps, act_steps = sem("dve_steps"), sem("act_steps")
        angle_ready, trig_ready = sem("angle_ready"), sem("trig_ready")
        proj_done, q_raw_ready, rot_done, rope_ready, evac_done = map(sem, (
            "proj_done", "q_raw_ready", "rot_done", "rope_ready", "evac_done"))
        va_done, va_ready = sem("va_done"), sem("va_ready")
        pair_used = sem("pair_used")
        masks_ready, early_in, early_ready = sem("masks_ready"), sem("early_in"), sem("early_ready")
        swa_scored, max_ready, swa_exp, prob_ready, probT_done, probT_ready, oa_done, oa_out = map(sem, (
            "swa_scored", "max_ready", "swa_exp", "prob_ready", "probT_done", "probT_ready", "oa_done", "oa_out"))
        sb_scored, abs_ready, log_ready, sp_ready, sb_summed, at_ready, ob_done, ob_out = map(sem, (
            "sb_scored", "abs_ready", "log_ready", "sp_ready", "sb_summed", "at_ready", "ob_done", "ob_out"))
        gate_done, sig_ready, up_done, merged_ready = map(sem, ("gate_done", "sig_ready", "up_done", "merged_ready"))
        out_done, x_ready = sem("out_done"), sem("x_ready")
        w_hi, w_split, y_hi, y_split, h1_hi, h1_split, m_hi, m_split = map(sem, (
            "w_hi", "w_split", "y_hi", "y_split", "h1_hi", "h1_split", "m_hi", "m_split"))
        qry_done, qry_ready, score_done, score_ready, score_used = map(sem, (
            "qry_done", "qry_ready", "score_done", "score_ready", "score_used"))
        best_ready, best_exp, slots_ready, slotsT_done, slotsT_ready = map(sem, (
            "best_ready", "best_exp", "slots_ready", "slotsT_done", "slotsT_ready"))
        picks, picked, pick_summed = map(sem, ("picks", "picked", "pick_summed"))
        hot_ready = [sem("hot_ready0"), sem("hot_ready1")]
        hot_done = [sem("hot_done0"), sem("hot_done1")]
        staged = [sem("staged0"), sem("staged1")]
        g_out = [sem("g_out0"), sem("g_out1")]
        stage_free = [sem("stage_free0"), sem("stage_free1")]
        e_in = [sem(f"e_in{e}") for e in range(2)]
        u_in = [sem(f"u_in{e}") for e in range(RING)]
        v_in = [sem(f"v_in{e}") for e in range(RING)]
        g_in = [sem(f"g_in{e}") for e in range(RING)]
        e_out = [sem(f"e_out{e}") for e in range(2)]
        gelu_out = [sem(f"gelu_out{e}") for e in range(RING)]
        s_done, gelu_ready, w_ready, a_hi, v_done = map(sem, ("s_done", "gelu_ready", "w_ready", "a_hi", "v_done"))
        last_turn = (NK - EARLY) // RING - 1
        bank_final = sem("bank_final")
        q_hi, q_split = sem("q_hi"), sem("q_split")
        y_ready, y_out = sem("y_ready"), sem("y_out")

        def wait_unit(engine, t):
            kind, m, c = UNITS[t]
            if kind == "gate":
                engine.wait_ge(gate_done, 2 * m + c + 1 + FREE)
            else:
                engine.wait_ge(up_done if kind == "up" else out_done, m + 1)

        def start(engine, *sems):
            for s in sems:
                engine.sem_inc(s, FREE)

        block = ctx.enter_context(nc.Block())

        @block.sync
        def _(sp):
            sp.dma_start(sml[:], small).then_inc(smalls_in, 16)
            sp.dma_start(cst[:], consts).then_inc(smalls_in, 16)
            sp.dma_start(ang.bitcast(I32), pos.to_broadcast([P, T])).then_inc(smalls_in, 16)
            sp.dma_start(x[:], xT).then_inc(x_in, 16)
            for n in range(4):
                sp.dma_start(ring[:, n, :], w_ada[n]).then_inc(ring_in[n], 16)
            sp.dma_start(kavaw, w_kava).then_inc(kava_in, 16)
            sp.wait_ge(ring_free[2], 1 + FREE)
            with sp.Fori(0, PAIRS) as i:
                for a in range(2):
                    sp.wait_ge(ring_free[a], i + 1 + FREE)
                    sp.dma_start(ring[:, a, :], row(w_ada, i * 2 + (4 + a))).then_inc(ring_in[a], 16)
                sp.wait_ge(gate_done, i * 2 + FREE)
                sp.dma_start(ring[:, 2, 0:2048], row(w_gate, i)).then_inc(early_in, 16)
            for s in range(4):
                sp.wait_ge(ring_free[s], ADA[s] + FREE)
            for s in range(4):
                sp.dma_start(wraw[:, s, :], w_units[s]).then_inc(ring_in[s], 16)
            with sp.Fori(1, len(UNITS) // 4) as r:
                for s in range(4):
                    sp.wait_ge(w_split, r * 4 + (s - 3))
                    sp.dma_start(wraw[:, s, :], row(w_units, r * 4 + s)).then_inc(ring_in[s], 16)
            sp.wait_ge(out_done, DC)
            sp.dma_start(skt, skT).then_inc(sk_in, 16)
            for s in range(2):
                sp.dma_start(ring[:, 2 + s, 0:2048], w_qry[s]).then_inc(ring_in[2 + s], 16)
                sp.dma_start(ute[:, s, :], euT[s]).then_inc(e_in[s], 16)
            with sp.Fori(1, HEADS // 2) as r:
                for s in range(2):
                    sp.wait_ge(q_split, r * 2 + (s - 1))
                    sp.dma_start(ring[:, 2 + s, 0:2048], row(w_qry, r * 2 + s)).then_inc(ring_in[2 + s], 16)
                    sp.wait_ge(s_done, r * 2 + (s - 1) + FREE)
                    sp.dma_start(ute[:, s, :], row(euT, r * 2 + s)).then_inc(e_in[s], 16)
            for n in range(HEADS, EARLY):
                sp.wait_ge(s_done, n - 1 + FREE)
                sp.dma_start(ute[:, n % 2, :], euT[n]).then_inc(e_in[n % 2], 16)

            sp.wait_ge(slotsT_ready, 3)
            for e in range(RING):
                sp.dma_start(ut[:, e, :], euT[EARLY + e]).then_inc(u_in[e], 16)
            with sp.Fori(1, (NK - EARLY) // RING) as r:
                for e in range(RING):
                    sp.wait_ge(u_split, r * RING + (e + 1 - RING))
                    sp.dma_start(ut[:, e, :], row(euT, r * RING + (EARLY + e))).then_inc(u_in[e], 16)
            for c in range(2):
                sp.wait_ge(g_out[c], 32 * (T // 128))

            def load_v(r, first):
                for e in range(RING):
                    n = r * RING + e
                    if not first:
                        sp.wait_ge(v_split, r * RING + (e + 1 - RING))
                    sp.dma_start(vt[:, e, :], row(ev, n)).then_inc(v_in[e], 16)
                    if not first:
                        sp.wait_ge(w_ready, r * RING + (e + 1 - RING))
                    sp.dma_start(gt[:, e, :], row(gates_dram, n)).then_inc(g_in[e], 16)
                    if first:
                        sp.wait_ge(e_out[e % 2], 16 * EARLY // 2 + FREE)
                    sp.dma_start(gl[:, e, :], row(gelu_dram, n)).then_inc(g_in[e], 16)

            load_v(0, True)
            for r in range(1, EARLY // RING):
                load_v(r, False)
            with sp.Fori(EARLY // RING, NK // RING) as r:
                for e in range(RING):
                    sp.wait_ge(gelu_out[e], (r - (EARLY // RING - 1)) * 16 + FREE)
                load_v(r, False)
            for k in range(0, DC, 2):
                sp.wait_ge(y_ready, k + 2)
                sp.dma_start(outT[:, k:k + 2, :], h[:, k:k + 2, :]).then_inc(y_out, 16)
            sp.wait_ge(y_out, 16 * DC // 2)

        @block.gpsimd
        def _(pool):
            start(pool, *stage_free)
            pool.wait_ge(ring_in[3], 16)
            with pool.Fori(0, PAIRS) as i:
                pool.wait_ge(pair_used, i + FREE)
                pool.dma_start(pairw.rearrange("p k n -> p (k n)"), row(w_pair, i)).then_inc(pair_in, 16)
            def query_low(n, s):
                pool.wait_ge(q_hi, n + 1)
                nc.gpsimd.tensor_tensor(q_parts[s][1], ring[:, 2 + s, 0:2048], q_parts[s][0].bitcast(F32),
                                        ALU.subtract).then_inc(q_split, 1)

            def index_picks(n):
                for c in range(2):
                    pool.wait_ge(picks, n * 2 + (c + 1))
                    p4 = pick[:, c, :, :].rearrange("p (t s) k -> p t s k", t=TT)
                    nc.gpsimd.tensor_tensor(p4, p4, tif[:, c, :, :].unsqueeze(2).to_broadcast([P, TT, TOPK, TOPK]),
                                            ALU.mult).then_inc(picked, 1)

            query_low(0, 0)
            query_low(1, 1)
            with pool.Fori(0, HEADS // 2 - 1) as r:
                for s in range(2):
                    query_low(r * 2 + (s + 2), s)
                    index_picks(r * 2 + s)
            for n in (HEADS - 2, HEADS - 1):
                index_picks(n)
            with pool.Fori(0, T // 128) as q:
                for c in range(2):
                    for b in range(2):
                        pool.wait_ge(staged[b], q * 16 + (8 * c + 8) + FREE)
                    for i0 in range(0, NK, NK // 2):
                        pool.dma_start(gates_dram[i0:i0 + NK // 2, :, bass.ds(q * 128 + c * 64, 64)].rearrange("i j t -> j i t"),
                                       stages[c][:, i0:i0 + NK // 2, :]).then_inc(g_out[c], 16)
                    pool.wait_ge(g_out[c], q * 32 + 32)
                    pool.sem_inc(stage_free[c], 1)

        @block.tensor
        def _(pe):
            start(pe, pair_used, gate_done, *hot_done, qry_done, score_done, s_done, v_done)
            def rms_sum(first, squares, chunks=range(DC)):
                for k in chunks:
                    pe.wait_ge(sq_ready, first + k + 1)
                    pe.matmul(ps[SUM_BANKS[first // DC]][:], ones, squares[:, k % 2, :], start=(k == 0), stop=(k == DC - 1)).then_inc(sq_summed, 1)

            def ada_sum(n, b, bank, col):
                pe.wait_ge(ada_ready, n + 1)
                for m in range(4):
                    last = pe.matmul(bank[:, bass.ds(col + m, 1)], adap[:, b, m * P:(m + 1) * P], ones[:, 0:1], start=True, stop=True)
                last.then_inc(ada_summed, 1)

            rms_sum(0, spl)
            for n in range(2):
                ada_sum(n, n % 2, ps[6], n * 4)
            pe.wait_ge(cact_ready, 1)
            pe.wait_ge(ring_in[2], 16)
            for m in range(4):
                for k in range(DC):
                    last = pe.matmul(ps[6][:, 8 + m:9 + m], ring[:, 2, k * 512 + m * P:k * 512 + (m + 1) * P], cact[:, k:k + 1],
                                     start=(k == 0), stop=(k == DC - 1))
            last.then_inc(ada_direct, 1)
            ada_sum(2, 0, ps[6], 12)
            pe.wait_ge(h_ready, DC)
            pe.wait_ge(kava_in, 16)
            for k in range(DC):
                last = pe.matmul(ps[0][:], kavaw[:, k, 0:P], h[:, k, :], start=(k == 0), stop=(k == DC - 1))
            last.then_inc(proj_done, 1)
            for t in range(TT):
                for k in range(DC):
                    last = pe.matmul(ps[1][:, t * P:(t + 1) * P], h[:, k, t * P:(t + 1) * P], kavaw[:, k, P:2 * P],
                                     start=(k == 0), stop=(k == DC - 1))
            last.then_inc(va_done, 1)
            pe.wait_ge(q_raw_ready, 1)
            pe.matmul(ps[4][:], cst[:, K_ROT:K_ROT + P], qraw, start=True, stop=True).then_inc(rot_done, 1)
            pe.wait_ge(va_ready, 1)
            pe.wait_ge(rope_ready, 1)
            pe.wait_ge(masks_ready, 1)

            with pe.Fori(0, PAIRS) as i:
                pe.wait_ge(pair_in, i * 16 + 16)
                pe.wait_ge(oa_out, i * 2 + FREE)
                pe.wait_ge(ob_out, i * 2 + FREE)
                pe.wait_ge(early_ready, i * 2 + FREE)
                for c in range(3):
                    for k in range(DC):
                        last = pe.matmul(ps[c][:], pairw[:, k, c * P:(c + 1) * P], h[:, k, :], start=(k == 0), stop=(k == DC - 1))
                    last.then_inc(proj_done, 1)
                for t in range(TT):
                    for k in range(DC):
                        last = pe.matmul(ps[3][:, t * P:(t + 1) * P], h[:, k, t * P:(t + 1) * P], pairw[:, k, 3 * P:4 * P],
                                         start=(k == 0), stop=(k == DC - 1))
                last.then_inc(proj_done, 1)
                pe.wait_ge(proj_done, i * 4 + 5)
                pe.sem_inc(pair_used, 1)
                for a in range(2):
                    ada_sum(i * 2 + (3 + a), 1 - a, ps[7], i * 8 + 4 * a)
                pe.wait_ge(q_raw_ready, i + 2)
                pe.wait_ge(at_ready, i * 8 + FREE)
                pe.matmul(ps[4][:], cst[:, K_ROT:K_ROT + P], qraw, start=True, stop=True).then_inc(rot_done, 1)
                pe.wait_ge(evac_done, i * 3 + 3)
                pe.wait_ge(rope_ready, i + 2)
                for a in range(2):
                    lo, hi = a * HD, (a + 1) * HD
                    for t in range(TT):
                        at = ps[t // 2][:, (t % 2) * 256:(t % 2) * 256 + 256]
                        if t == 0:
                            pe.matmul(at[:, 0:P], ident_r, never_r, start=True, stop=True)
                            pe.matmul(at[:, P:2 * P], ident_r, window_r[:, P:2 * P], start=True, stop=False)
                        else:
                            pe.matmul(at, ident_r, window_r, start=True, stop=False)
                        if t == 0:
                            last = pe.matmul(at[:, P:2 * P], qR[lo:hi, 0:P], kR[lo:hi, 0:P], start=False, stop=True)
                        else:
                            last = pe.matmul(at, qR[lo:hi, t * P:(t + 1) * P], kR[lo:hi, (t - 1) * P:(t + 1) * P],
                                             start=False, stop=True)
                    last.then_inc(swa_scored, 1)
                    pe.wait_ge(at_ready, i * 8 + a * 4 + FREE)
                    for b in range(4):
                        pe.matmul(ps[4 + b][:, b * P:T], kB[lo:hi, b * P:(b + 1) * P], qB[lo:hi, b * P:T],
                                  start=True, stop=True).then_inc(sb_scored, 1)
                    pe.wait_ge(early_in, i * 16 + 16)
                    pe.wait_ge(early_ready, i * 2 + a + FREE)
                    for k in range(DC):
                        last = pe.matmul(ps[2][:], ring[:, 2, k * 256 + a * P:k * 256 + (a + 1) * P], h[:, k, :],
                                         start=(k == 0), stop=(k == DC - 1))
                    last.then_inc(gate_done, 1)
                    pe.wait_ge(prob_ready, i * 2 + (a + 1))
                    for t in range(TT):
                        for c in range(2):
                            last = pe.transpose(ps[1 + t // 2 * 2][:, (t % 2) * 256 + c * P:(t % 2) * 256 + (c + 1) * P],
                                                prob[:, t, c * P:(c + 1) * P], ident)
                    last.then_inc(probT_done, 1)
                    pe.wait_ge(sp_ready, i * 8 + (a * 4 + 4))
                    for b in range(4):
                        pe.matmul(ps[4 + b][:, b * P:T], cst[:, K_NTRI:K_NTRI + P], spl[:, b, b * P:T], start=False, stop=False,
                                  skip_group_check=True)
                        for c in range(b + 1, 4):
                            pe.matmul(ps[4 + b][:, c * P:T], cst[:, K_NONE:K_NONE + P], spl[:, c, c * P:T], start=False, stop=False,
                                      skip_group_check=True)
                        pe.matmul(ps[4 + b][:, b * P:(b + 1) * P], ident_r, after_r, start=False, stop=True,
                                  skip_group_check=True).then_inc(sb_summed, 1)
                    pe.wait_ge(probT_ready, i * 2 + (a + 1))
                    for t in range(TT):
                        for c in ((1,) if t == 0 else (0, 1)):
                            last = pe.matmul(ps[0][lo:hi, t * P:(t + 1) * P], vA[:, t - 1 + c, lo:hi],
                                             probT[:, t, c * P:(c + 1) * P], start=(c == 0 or t == 0), stop=(c == 1))
                    last.then_inc(oa_done, 1)
                    for b in range(4):
                        pe.wait_ge(at_ready, i * 8 + (a * 4 + b + 1) + FREE)
                        last = pe.matmul(ps[1][lo:hi, b * P:T], vB[:, b, lo:hi], atB[:, b, b * P:T], start=(b == 0), stop=(b == 3),
                                         skip_group_check=True)
                    last.then_inc(ob_done, 1)
                    if a == 0:
                        pe.wait_ge(oa_out, i * 2 + 1 + FREE)
                        pe.wait_ge(ob_out, i * 2 + 1 + FREE)

            pe.wait_ge(oa_out, 2 * PAIRS + FREE)
            pe.wait_ge(ob_out, 2 * PAIRS + FREE)
            pe.wait_ge(mod_ready, 2)
            pe.wait_ge(early_ready, 2 * PAIRS + FREE)
            for t, (kind, m, c) in enumerate(UNITS):
                pe.wait_ge(w_split, t + 1)
                if kind == "out":
                    if m >= 2:
                        pe.wait_ge(x_ready, m - 1)
                    if m < 2:
                        pe.wait_ge(merged_ready, DC - 1 + FREE)
                elif m >= 2 and c == 0:
                    pe.wait_ge(merged_ready, m - 1 + FREE)
                if kind == "gate" and m == 4 and c == 0:
                    pe.wait_ge(h1_split, DC)
                x_split = {"up": ys, "gate": h1s, "out": ms}[kind]
                for k in range(DC):
                    if t == 0:
                        pe.wait_ge(y_split, k + 1)
                    if kind == "out":
                        bank, first, end = m % 2, k == 0, k == DC - 1
                        if m == 0:
                            pe.wait_ge(m_split, k + 1)
                    elif kind == "gate":
                        bank, first, end = 4 * (m % 2) + c, k == 0, k == DC - 1
                    else:
                        bank, first, end = 4 * (m % 2) + 2 + k // PAIRS, k % PAIRS == 0, k % PAIRS == PAIRS - 1
                    for q, (wp, xp) in enumerate(PASSES):
                        last = pe.matmul(ps[bank][:], ws[:, t % 2, wp, k * P:(k + 1) * P], x_split[:, xp, k, :],
                                         start=(first and q == 0), stop=(end and q == 2))
                last.then_inc({"up": up_done, "gate": gate_done, "out": out_done}[kind], 1)
                if kind == "out" and m:
                    rms_sum(DC, squares2, [m - 1])
            rms_sum(DC, squares2, [DC - 1])
            pe.wait_ge(sk_in, 16)
            with pe.Fori(0, HEADS // 2) as r:
                for s in range(2):
                    pe.wait_ge(q_split, r * 2 + (s + 1))
                    pe.wait_ge(qry_ready, r * 4 + s * 2 + FREE)
                    for c in range(2):
                        for k in range(DC):
                            if s == 0 and c == 0:
                                pe.wait_ge(h_split, k + 1)
                            for q, (wp, xp) in enumerate(PASSES):
                                last = pe.matmul(ps[c][:], q_parts[s][wp][:, k * 256 + c * P:k * 256 + (c + 1) * P], hs[:, xp, k, :],
                                                 start=(k == 0 and q == 0), stop=(k == DC - 1 and q == 2))
                        last.then_inc(qry_done, 1)
                    pe.wait_ge(qry_ready, r * 4 + (s * 2 + 2) + FREE)
                    pe.wait_ge(score_ready, r * 4 + s * 2 + FREE)
                    for c in range(2):
                        for t in range(TT):
                            last = pe.matmul(ps[2 + c][:, t * P:(t + 1) * P], qv[:, c, t * P:(t + 1) * P],
                                             skt[:, bass.ds(r * 4 + (s * 2 + c), 1), :].rearrange("p a n -> p (a n)"), start=True, stop=True)
                        last.then_inc(score_done, 1)
                    pe.wait_ge(e_in[s], r * 16 + 16)
                    pe.wait_ge(gelu_ready, r * 2 + FREE)
                    for k in range(DC):
                        last = pe.matmul(ps[4 + s][:], ute[:, s, k * P:(k + 1) * P], h[:, k, :], start=(k == 0), stop=(k == DC - 1))
                    last.then_inc(s_done, 1)
            def early_scores(n):
                pe.wait_ge(e_in[n % 2], n // 2 * 16 + 16)
                pe.wait_ge(gelu_ready, min(n - 1, HEADS) + FREE)
                for k in range(DC):
                    last = pe.matmul(ps[4 + n % 4][:], ute[:, n % 2, k * P:(k + 1) * P], h[:, k, :], start=(k == 0), stop=(k == DC - 1))
                last.then_inc(s_done, 1)

            for n in range(HEADS, EARLY - 1):
                early_scores(n)
            pe.wait_ge(pick_summed, 2 * HEADS + FREE)
            pe.wait_ge(slots_ready, HEADS)
            pe.wait_ge(score_ready, 2 * HEADS + FREE)
            for f in range(3):
                for t in range(TT):
                    last = pe.transpose(ps[f][:, t * P:(t + 1) * P], slots[:, f, t, :], ident)
                last.then_inc(slotsT_done, 1)
            early_scores(EARLY - 1)
            pe.wait_ge(slotsT_ready, 3)

            def scores(r, e):
                pe.wait_ge(u_split, r * RING + (e + 1))
                pe.wait_ge(gelu_ready, r * RING + (EARLY + e - 1) + FREE)
                for k in range(DC):
                    for q, (wp, xp) in enumerate(PASSES):
                        last = pe.matmul(ps[e % 2][:], us[:, e % 2, wp, k * P:(k + 1) * P], hs[:, xp, k, :],
                                         start=(k == 0 and q == 0), stop=(k == DC - 1 and q == 2))
                last.then_inc(s_done, 1)

            with pe.Fori(0, WITH_G // RING) as r:
                for e in range(RING):
                    scores(r, e)
                    for b in range(2):
                        pe.wait_ge(hot_ready[b], r * 32 + (8 * e + 8))
                        pe.wait_ge(staged[b], r * 4 + e + FREE)
                        for q in range(4):
                            last = pe.matmul(ps[2 + b][:, q * P:(q + 1) * P], ohj[:, b, q, :], ohi[:, b, q, :], start=True, stop=True)
                        last.then_inc(hot_done[b], 1)
            with pe.Fori(WITH_G // RING, (NK - EARLY) // RING) as r:
                for e in range(RING):
                    scores(r, e)

            def values(r, e, first=False, final=False):
                pe.wait_ge(v_split, r * RING + (e + 1))
                pe.wait_ge(a_split, r * RING + (e + 1))
                for k in range(DC):
                    for q, (wp, xp) in enumerate(PASSES):
                        last = pe.matmul(ps[k][:], vs[:, e % 2, wp, k * P:(k + 1) * P], ar[:, e % 2, xp, :],
                                         start=(first and q == 0), stop=True, skip_group_check=True)
                    if final:
                        last.then_inc(bank_final, 1)
                if not final:
                    last.then_inc(v_done, 1)

            pe.wait_ge(gelu_ready, NK + FREE)
            for e in range(RING):
                values(0, e, first=(e == 0))
            with pe.Fori(1, NK // RING - 1) as r:
                for e in range(RING):
                    values(r, e)
            for e in range(RING):
                values(NK // RING - 1, e, final=(e == RING - 1))
            rms_sum(2 * DC, squares3)

        @block.scalar
        def _(sa):
            start(sa, at_ready, qry_ready, score_ready, gelu_ready, *staged, *e_out, *gelu_out)
            act_ = nc.scalar.activation

            def squares(first, dst, chunks=range(DC)):
                for k in chunks:
                    if k == DC - 1:
                        act_(tiny[:], cst[:, K_EPS:K_EPS + 1], ACT.Sqrt)
                    if first:
                        sa.wait_ge(x_ready, first - DC + k + 1)
                    if k >= 2:
                        sa.wait_ge(sq_summed, first + k - 1)
                    act_(dst[:, k % 2, :], x[:, k, :], ACT.Square).then_inc(sq_ready, 1)

            def root(n):
                sa.wait_ge(sq_summed, n * DC)
                act_(rstd[:], ps[SUM_BANKS[n - 1]][:], ACT.Sqrt, scale=1.0 / D, bias=cst[:, K_EPS:K_EPS + 1]).then_inc(root_ready, 1)

            def modulate(n, mul, shift, chunks=range(DC)):
                for k in chunks:
                    sa.wait_ge(norm_part, n * DC + k + 1)
                    act_(h[:, k, :], h[:, k, :], ACT.Identity, scale=mul[:, k:k + 1], bias=part(shift, k)).then_inc(h_ready, 1)

            sa.wait_ge(smalls_in, 48)
            act_(cact[:], sml[:, S_C:S_C + DC], ACT.Silu).then_inc(cact_ready, 1)
            sa.wait_ge(x_in, 16)
            squares(0, spl)
            root(1)
            sa.wait_ge(mod_ready, 1)
            modulate(0, mul1, 0)
            sa.wait_ge(angle_ready, 2)
            act_(sinT, sinT, ACT.Sin).then_inc(trig_ready, 1)
            act_(cosT, cosT, ACT.Sin).then_inc(trig_ready, 1)
            sa.wait_ge(proj_done, 1)
            act_(qraw, ps[0][:], ACT.Copy).then_inc(q_raw_ready, 1)
            sa.wait_ge(va_done, 1)
            act_(vA.rearrange("p a b -> p (a b)"), ps[1][:], ACT.Copy).then_inc(va_ready, 1)
            sa.wait_ge(rope_ready, 1)

            with sa.Fori(0, PAIRS) as i:
                sa.wait_ge(proj_done, i * 4 + 2)
                act_(qraw, ps[0][:], ACT.Copy, scale=HD ** -0.5).then_inc(q_raw_ready, 1)
                for c, dst in ((1, qB), (2, kB), (3, vB.rearrange("p a b -> p (a b)"))):
                    sa.wait_ge(proj_done, i * 4 + (2 + c))
                    act_(dst, ps[c][:], ACT.Copy, scale=HD ** -0.5 if c == 1 else 1.0).then_inc(evac_done, 1)
                for a in range(2):
                    for b in range(4):
                        sa.wait_ge(sb_scored, i * 8 + (a * 4 + b + 1))
                        act_(spl[:, b, b * P:T], ps[4 + b][:, b * P:T], ACT.Abs).then_inc(abs_ready, 1)
                    for b in range(4):
                        sa.wait_ge(abs_ready, i * 8 + (a * 4 + b + 1))
                        act_(spl[:, b, b * P:T], spl[:, b, b * P:T], ACT.Exp, scale=-1.0).then_inc(act_steps, 1)
                    sa.wait_ge(max_ready, i * 2 + (a + 1))
                    for t in range(TT):
                        act_(prob[:, t, :], ps[t // 2][:, (t % 2) * 256:(t % 2) * 256 + 256], ACT.Exp,
                             bias=mx[:, 4 + t:5 + t], accum_out=sk4[:, t:t + 1]).then_inc(swa_exp, 1)
                    act_(sk4[:, 4:8], mx[:, 4:8], ACT.Exp, bias=sml[:, bass.ds(i * 2 + (S_SINK + a), 1)]).then_inc(swa_exp, 1)
                    for b in range(4):
                        sa.wait_ge(act_steps, i * 8 + (a * 4 + b + 1))
                        act_(spl[:, b, b * P:T], spl[:, b, b * P:T], ACT.Ln, bias=1.0).then_inc(log_ready, 1)
                    sa.wait_ge(probT_done, i * 2 + (a + 1))
                    for c in range(2):
                        last = act_(probT[:, 2 * c:2 * c + 2, :].rearrange("p a b -> p (a b)"), ps[1 + 2 * c][:], ACT.Copy)
                    last.then_inc(probT_ready, 1)
                    for b in range(4):
                        sa.wait_ge(sb_summed, i * 8 + (a * 4 + b + 1))
                        act_(atB[:, b, b * P:T], ps[4 + b][:, b * P:T], ACT.Exp).then_inc(at_ready, 1)

            def unit_high(t):
                sa.wait_ge(ring_in[t % 4], 16 * (ADA[t % 4] + t // 4 + 1))
                if t >= 2:
                    wait_unit(sa, t - 2)
                act_(ws[:, t % 2, 0, :], wraw[:, t % 4, :], ACT.Copy).then_inc(w_hi, 1)

            def sigmoids(m):
                if m >= 2:
                    sa.wait_ge(merged_ready, m - 1 + FREE)
                for c, dst in enumerate((siga, sigb)):
                    if m < 4:
                        sa.wait_ge(early_ready, 2 * m + c + 1 + FREE)
                        gate = early_gates[:, 2 * m + c, :]
                    else:
                        sa.wait_ge(gate_done, 2 * m + c + 1 + FREE)
                        gate = ps[4 * (m % 2) + c][:]
                    act_(dst[:, m % 2, :], gate, ACT.Sigmoid).then_inc(sig_ready, 1)

            def merged_high(m):
                sa.wait_ge(merged_ready, m + 1 + FREE)
                act_(ms[:, 0, m, :], merged[:, m, :], ACT.Copy).then_inc(m_hi, 1)

            unit_high(0)
            unit_high(1)
            sa.wait_ge(oa_out, 2 * PAIRS + FREE)
            sa.wait_ge(ob_out, 2 * PAIRS + FREE)
            for k in range(2 * PAIRS):
                act_(ys[:, 0, k, :], y8[:, k, :], ACT.Copy).then_inc(y_hi, 1)
            for k in range(DC):
                act_(h1s[:, 0, k, :], h[:, k, :], ACT.Copy).then_inc(h1_hi, 1)
            for t, (kind, m, c) in enumerate(UNITS):
                if kind == "up":
                    sigmoids(m)
                if kind == "up" and m == DC - 1:
                    for k in range(DC - 1):
                        merged_high(k)
                    merged_high(m)
                if t + 2 < len(UNITS):
                    unit_high(t + 2)
                if kind == "out":
                    squares(DC, squares2, [m])
            def query_high(n, s):
                sa.wait_ge(ring_in[2 + s], (n - s) * 8 + (16 * ADA[2 + s] + 4 * len(UNITS) + 16))
                if not isinstance(n, int) or n >= 2:
                    sa.wait_ge(qry_done, n * 2 - 2 + FREE)
                act_(q_parts[s][0], ring[:, 2 + s, 0:2048], ACT.Copy).then_inc(q_hi, 1)

            root(2)
            query_high(0, 0)
            sa.wait_ge(mod_ready, 2)
            for k in range(DC):
                modulate(1, mul2, 3, [k])
                sa.wait_ge(h_ready, DC + k + 1)
                act_(hs[:, 0, k, :], h[:, k, :], ACT.Copy).then_inc(hi_ready, 1)
            query_high(1, 1)

            def copies(n):
                sa.wait_ge(score_done, n * 2 + FREE)
                for c in range(2):
                    sa.wait_ge(qry_done, n * 2 + (c + 1) + FREE)
                    act_(qv[:, c, :], ps[c][:], ACT.Copy).then_inc(qry_ready, 1)
                sa.wait_ge(score_used, n + FREE)
                for c in range(2):
                    sa.wait_ge(score_done, n * 2 + (c + 1) + FREE)
                    act_(sc[:, c, :, :].rearrange("p a b -> p (a b)"), ps[2 + c][:], ACT.Copy).then_inc(score_ready, 1)

            def head(n, s, more=True, split=True):
                sa.wait_ge(s_done, n + 1 + FREE)
                sa.wait_ge(e_out[s], (n - s) * 8 + FREE)
                act_(gele[:, s, :], ps[4 + s][:], ACT.Gelu).then_inc(gelu_ready, 1)
                sa.wait_ge(gelu_ready, n + 1 + FREE)
                sa.dma_start(row(gelu_dram, n), gele[:, s, :]).then_inc(e_out[s], 16)
                if split:
                    query_high(n + 2, s)
                if more:
                    copies(n + 1)
                sa.wait_ge(best_ready, n + 1)
                act_(bv.rearrange("p a b -> p (a b)"), bv.rearrange("p a b -> p (a b)"), ACT.Exp).then_inc(best_exp, 1)

            copies(0)
            with sa.Fori(0, HEADS // 2 - 1) as r:
                for s in range(2):
                    head(r * 2 + s, s)
            head(HEADS - 2, 0, split=False)
            head(HEADS - 1, 1, more=False, split=False)

            def early_gelu(n):
                sa.wait_ge(s_done, n + 1 + FREE)
                sa.wait_ge(e_out[n % 2], n // 2 * 16 + FREE)
                act_(gele[:, n % 2, :], ps[4 + n % 4][:], ACT.Gelu).then_inc(gelu_ready, 1)
                sa.wait_ge(gelu_ready, n + 1 + FREE)
                sa.dma_start(gelu_dram[n], gele[:, n % 2, :]).then_inc(e_out[n % 2], 16)

            for n in range(HEADS, EARLY - 1):
                early_gelu(n)
            for f in range(3):
                sa.wait_ge(slotsT_done, f + 1)
                act_(slotsT[:, f, :], ps[f][:], ACT.Copy).then_inc(slotsT_ready, 1)

            def u_high(r, e):
                sa.wait_ge(u_in[e], r * 16 + 16)
                act_(us[:, e % 2, 0, :], ut[:, e, :], ACT.Copy).then_inc(u_hi, 1)

            def gelus(r, e, ahead=True):
                sa.wait_ge(s_done, r * RING + (EARLY + e + 1) + FREE)
                sa.wait_ge(gelu_out[e], r * 16 + FREE)
                act_(gel[:, e, :], ps[e % 2][:], ACT.Gelu).then_inc(gelu_ready, 1)
                if ahead:
                    u_high(r + (e + 2) // RING, (e + 2) % RING)
                sa.wait_ge(gelu_ready, r * RING + (EARLY + e + 1) + FREE)
                sa.dma_start(row(gelu_dram, r * RING + (EARLY + e)), gel[:, e, :]).then_inc(gelu_out[e], 16)

            u_high(0, 0)
            u_high(0, 1)
            early_gelu(EARLY - 1)
            for c in range(2):
                sa.wait_ge(e_out[c], 16 * EARLY // 2 + FREE)
            with sa.Fori(0, T // 128) as q:
                for c in range(2):
                    sa.wait_ge(stage_free[c], q + FREE)
                    with sa.Fori(0, 2) as r:
                        for e in range(RING):
                            gelus(q * 4 + r + 2 * c, e)
                            for b in range(2):
                                sa.wait_ge(hot_done[b], q * 16 + r * 4 + (8 * c + e + 1) + FREE)
                                act_(stages[c][:, :, bass.ds(r * 32 + (e * 8 + b * 4), 4)],
                                     ps[2 + b][:].rearrange("p (t i) -> p i t", t=4), ACT.Copy).then_inc(staged[b], 1)
            with sa.Fori(WITH_G // RING, last_turn) as r:
                for e in range(RING):
                    gelus(r, e)
            def v_high(r, e):
                sa.wait_ge(v_in[e], r * 16 + 16)
                if not isinstance(r, int) or e >= 2:
                    sa.wait_ge(v_done, r * RING + (e - 1) + FREE)
                act_(vs[:, e % 2, 0, :], vt[:, e, :], ACT.Copy).then_inc(v_hi, 1)

            for e in range(RING):
                gelus(last_turn, e, ahead=(e < 2))
                if e < 2:
                    v_high(0, e)
            for e in range(2, RING):
                v_high(0, e)
            with sa.Fori(1, NK // RING) as r:
                for e in range(RING):
                    v_high(r, e)
            squares(2 * DC, squares3)
            root(3)

        @block.vector
        def _(ve):
            start(ve, pick_summed, early_ready, *ring_free, oa_out, ob_out, merged_ready, score_used)
            nv = nc.vector
            step = Steps(ve, dve_steps)
            step.pad = pad[:]

            def inv_rms(n):
                ve.wait_ge(root_ready, n)
                step(nv.reciprocal(rstd[:], rstd[:]))

            def ada_product(n, slot, b, loads):
                ve.wait_ge(ring_in[slot], loads * 16)
                if not isinstance(n, int) or n >= 2:
                    ve.wait_ge(ada_summed, n - 1)
                w = ring[:, slot, :].rearrange("p (k n) -> p k n", k=DC)
                step(nv.tensor_scalar(adap[:, b, :], w[:, 0, :], cact[:, 0:1], None, ALU.mult))
                for k in range(1, DC):
                    ins = nv.scalar_tensor_tensor(adap[:, b, :], w[:, k, :], cact[:, k:k + 1], adap[:, b, :], ALU.mult, ALU.add)
                    if k < DC - 1:
                        step(ins)
                ins.then_inc(ada_ready, 1)
                ve.wait_ge(ada_ready, n + 1)
                ve.sem_inc(ring_free[slot], 1)

            ve.wait_ge(smalls_in, 48)
            ve.wait_ge(cact_ready, 1)
            for n in range(2):
                ada_product(n, n, n % 2, 1)
            inv_rms(1)
            for k in range(DC):
                ve.wait_ge(x_in, 16)
                nv.tensor_tensor(h[:, k, :], x[:, k, :], rstd[:], ALU.mult).then_inc(norm_part, 1)
            ada_product(2, 3, 0, 1)
            ve.wait_ge(ada_direct, 1)
            ve.sem_inc(ring_free[2], 1)
            for dst, col in ((ident_r, K_ID), (window_r, K_SWA), (never_r, K_NEVER), (after_r, K_SBM)):
                ins = nv.tensor_copy(dst, cst[:, col:col + dst.shape[-1]])
            ins.then_inc(masks_ready, 1)
            ve.wait_ge(ada_summed, 3)
            step(nv.tensor_tensor(mod[:, 0:16], ps[6][:, 0:16], sml[:, S_B:S_B + 16], ALU.add))
            nv.scalar_tensor_tensor(mul1[:], part(1), 1.0, sml[:, S_G1:S_G1 + DC], ALU.add, ALU.mult).then_inc(mod_ready, 1)

            step(nv.tensor_copy(turn, ang.bitcast(I32)))
            step(nv.tensor_scalar(ang, turn, cst[:, K_INV:K_INV + 1], None, ALU.mult))
            for dst, quarter in ((sinT, 0.0), (cosT, 0.25)):
                step(nv.tensor_scalar(turn, ang, 1 / TWO_PI, quarter, ALU.mult, ALU.add))
                step(nv.tensor_scalar(turn, turn, MAGIC, None, ALU.add))
                step(nv.tensor_scalar(turn, turn, -MAGIC, None, ALU.add))
                step(nv.scalar_tensor_tensor(dst, turn, -C1, ang, ALU.mult, ALU.add))
                step(nv.scalar_tensor_tensor(dst, turn, -C2, dst, ALU.mult, ALU.add))
                step(nv.scalar_tensor_tensor(dst, turn, -C3, dst, ALU.mult, ALU.add))
                step(nv.tensor_scalar(dst, dst, quarter * TWO_PI, None, ALU.add))
                nv.tensor_scalar(dst, dst, -3.1415925, 3.1415925, ALU.max, ALU.min).then_inc(angle_ready, 1)
            def rope(n, dst):
                ve.wait_ge(q_raw_ready, n)
                step(nv.tensor_tensor(dst, qraw, cosT, ALU.mult))
                ve.wait_ge(rot_done, n)
                step(nv.tensor_tensor(ang, ps[4][:], sinT, ALU.mult))
                nv.tensor_tensor(dst, dst, ang, ALU.add).then_inc(rope_ready, 1)

            ve.wait_ge(trig_ready, 2)
            rope(1, kR)

            with ve.Fori(0, PAIRS) as i:
                step.enter(i, 24)
                for a in range(2):
                    ada_product(i * 2 + (3 + a), a, 1 - a, i + 2)
                rope(i + 2, qR)
                for a in range(2):
                    lo, hi = a * HD, (a + 1) * HD
                    ve.wait_ge(swa_scored, i * 2 + (a + 1))
                    for c in range(2):
                        ins = nv.tensor_reduce(mx[:, 2 * c:2 * c + 2], ps[c][:].rearrange("p (a b) -> p a b", a=2), AX.X, ALU.max)
                    step(ins)
                    nv.tensor_scalar(mx[:, 4:8], mx[:, 0:4], sml[:, bass.ds(i * 2 + (S_SINK + a), 1)], -1.0,
                                     ALU.max, ALU.mult).then_inc(max_ready, 1)
                    ve.wait_ge(swa_exp, i * 10 + (a * 5 + 5))
                    step(nv.tensor_tensor(sk4[:, 8:12], sk4[:, 0:4], sk4[:, 4:8], ALU.add))
                    step(nv.reciprocal(sk4[:, 12:16], sk4[:, 8:12]))
                    for t in range(TT):
                        ins = nv.tensor_scalar(prob[:, t, :], prob[:, t, :], sk4[:, 12 + t:13 + t], None, ALU.mult)
                    ins.then_inc(prob_ready, 1)
                    for b in range(4):
                        ve.wait_ge(log_ready, i * 8 + (a * 4 + b + 1))
                        ins = nv.scalar_tensor_tensor(spl[:, b, b * P:T], ps[4 + b][:, b * P:T], 0.0, spl[:, b, b * P:T],
                                                      ALU.max, ALU.add)
                    step(ins)
                    for b in range(4):
                        nv.tensor_tensor(spl[:, b, b * P:(b + 1) * P], spl[:, b, b * P:(b + 1) * P], cst[:, K_CAUS:K_CAUS + P],
                                         ALU.mult).then_inc(sp_ready, 1)
                    ve.wait_ge(gate_done, i * 2 + (a + 1) + FREE)
                    nv.tensor_copy(early_gates[:, bass.ds(i * 2 + a, 1), :].rearrange("p a n -> p (a n)"), ps[2][:]).then_inc(early_ready, 1)
                    ve.wait_ge(oa_done, i * 2 + (a + 1))
                    nv.tensor_copy(yA[lo:hi, bass.ds(i, 1), :].rearrange("p a n -> p (a n)"), ps[0][lo:hi, :]).then_inc(oa_out, 1)
                    ve.wait_ge(ob_done, i * 2 + (a + 1))
                    nv.tensor_copy(yB[lo:hi, bass.ds(i, 1), :].rearrange("p a n -> p (a n)"), ps[1][lo:hi, :]).then_inc(ob_out, 1)
                step.leave(PAIRS)

            ve.wait_ge(ada_summed, 11)
            step(nv.tensor_tensor(mod[:, 16:48], ps[7][:, 0:32], sml[:, S_B + 16:S_B + 48], ALU.add))
            nv.scalar_tensor_tensor(mul2[:], part(4), 1.0, sml[:, S_G2:S_G2 + DC], ALU.add, ALU.mult).then_inc(mod_ready, 1)
            def unit_low(t):
                ve.wait_ge(w_hi, t + 1)
                nv.tensor_tensor(ws[:, t % 2, 1, :], wraw[:, t % 4, :], ws[:, t % 2, 0, :].bitcast(F32), ALU.subtract).then_inc(w_split, 1)

            def merged_low(m):
                ve.wait_ge(m_hi, m + 1)
                nv.tensor_tensor(ms[:, 1, m, :], merged[:, m, :], ms[:, 0, m, :].bitcast(F32), ALU.subtract).then_inc(m_split, 1)

            unit_low(0)
            unit_low(1)
            for k in range(2 * PAIRS):
                ve.wait_ge(y_hi, k + 1)
                nv.tensor_tensor(ys[:, 1, k, :], y8[:, k, :], ys[:, 0, k, :].bitcast(F32), ALU.subtract).then_inc(y_split, 1)
            for k in range(DC):
                ve.wait_ge(h1_hi, k + 1)
                nv.tensor_tensor(h1s[:, 1, k, :], h[:, k, :], h1s[:, 0, k, :].bitcast(F32), ALU.subtract).then_inc(h1_split, 1)
            for t, (kind, m, c) in enumerate(UNITS):
                if t + 2 < len(UNITS) and (kind, m) != ("up", DC - 1):
                    unit_low(t + 2)
                if kind == "up":
                    b = m % 2
                    if m == DC - 1:
                        for k in range(DC - 1):
                            merged_low(k)
                    ve.wait_ge(sig_ready, 2 * m + 2)
                    ve.wait_ge(up_done, m + 1)
                    nv.tensor_tensor(ma[:, b, :], siga[:, b, :], ps[4 * b + 2][:], ALU.mult)
                    step(nv.tensor_tensor(mb[:, b, :], sigb[:, b, :], ps[4 * b + 3][:], ALU.mult))
                    nv.tensor_tensor(merged[:, m, :], ma[:, b, :], mb[:, b, :], ALU.add).then_inc(merged_ready, 1)
                    if m == DC - 1:
                        merged_low(m)
                        unit_low(t + 2)
                if kind == "out":
                    ve.wait_ge(out_done, m + 1)
                    nv.scalar_tensor_tensor(x[:, m, :], ps[m % 2][:], part(2, m), x[:, m, :], ALU.mult, ALU.add).then_inc(x_ready, 1)
            inv_rms(2)
            for k in range(DC):
                nv.tensor_tensor(h[:, k, :], x[:, k, :], rstd[:], ALU.mult).then_inc(norm_part, 1)

            for k in range(DC):
                ve.wait_ge(hi_ready, k + 1)
                nv.tensor_tensor(hs[:, 1, k, :], h[:, k, :], hs[:, 0, k, :].bitcast(F32), ALU.subtract).then_inc(h_split, 1)

            def finish(i):
                ve.wait_ge(best_exp, i + 1)
                step(nv.tensor_reduce(den[:, 0:TT], bv, AX.X, ALU.add))
                step(nv.reciprocal(den[:, TT:2 * TT], den[:, 0:TT]))
                nv.tensor_tensor(slots[:, 2, :, bass.ds(i * TOPK, TOPK)], bv, den[:, TT:2 * TT].unsqueeze(2).to_broadcast([P, TT, TOPK]),
                                 ALU.mult).then_inc(slots_ready, 1)
                for c in range(2):
                    ve.wait_ge(picked, i * 2 + (c + 1))
                    nv.tensor_reduce(slots[:, c, :, bass.ds(i * TOPK, TOPK)], pick[:, c, :, :].rearrange("p (t s) k -> p t s k", t=TT),
                                     AX.X, ALU.add).then_inc(pick_summed, 1)

            def rank(i, finish_before=False):
                step.wait_apart(score_ready, i * 2 + 2 + FREE)
                every = [(c, t) for c in range(2) for t in range(TT)]

                for c, t in every:
                    ins = nv.max(tv[:, c, t, 0:8], sc[:, c, t, :])
                step(ins, apart=True)
                for c, t in every:
                    nv.max_index(ti[:, c, t, 0:8], tv[:, c, t, 0:8], sc[:, c, t, :])
                    ins = nv.match_replace(sc2[:, c, t, :], tv[:, c, t, 0:8], sc[:, c, t, :], LOWEST)
                ins.then_inc(score_used, 1)
                step.wait_apart(score_used, i + 1 + FREE)
                for c, t in every:
                    ins = nv.max(tv[:, c, t, 8:16], sc2[:, c, t, :])
                step(ins, apart=True)
                for c, t in every:
                    nv.max_index(ti[:, c, t, 8:16], tv[:, c, t, 8:16], sc2[:, c, t, :])
                if finish_before:
                    finish(i - 1)
                nv.tensor_tensor(cand[:, :, 0:64].rearrange("p t (a b) -> p t a b", a=4),
                                 tv[:, 0, :, 0:4].unsqueeze(3).to_broadcast([P, TT, 4, TOPK]),
                                 tv[:, 1, :, :].unsqueeze(2).to_broadcast([P, TT, 4, TOPK]), ALU.add)
                ins = nv.tensor_tensor(cand[:, :, 64:CAND].rearrange("p t (a b) -> p t a b", a=12),
                                       tv[:, 0, :, 4:16].unsqueeze(3).to_broadcast([P, TT, 12, 4]),
                                       tv[:, 1, :, 0:4].unsqueeze(2).to_broadcast([P, TT, 12, 4]), ALU.add)
                step(ins, apart=True)
                for t in range(TT):
                    ins = nv.max(bv[:, t, 0:8], cand[:, t, :])
                step(ins, apart=True)
                for t in range(TT):
                    nv.max_index(bi[:, t, 0:8], bv[:, t, 0:8], cand[:, t, :])
                    ins = nv.match_replace(cand2[:, t, :], bv[:, t, 0:8], cand[:, t, :], LOWEST)
                step(ins, apart=True)
                for t in range(TT):
                    ins = nv.max(bv[:, t, 8:16], cand2[:, t, :])
                step(ins, apart=True)
                for t in range(TT):
                    ins = nv.max_index(bi[:, t, 8:16], bv[:, t, 8:16], cand2[:, t, :])
                nv.tensor_copy(den[:, 0:TT], bv[:, :, 0:1].rearrange("p a b -> p (a b)"))
                step(nv.tensor_copy(tif.rearrange("p a b c -> p (a b c)"), ti.rearrange("p a b c -> p (a b c)")))
                nv.tensor_tensor(bv, bv, den[:, 0:TT].unsqueeze(2).to_broadcast([P, TT, TOPK]), ALU.subtract).then_inc(best_ready, 1)
                bif = bi.rearrange("p a b -> p (a b)")
                nv.tensor_scalar(shifted[:, 0, :], bif, 4, None, ALU.logical_shift_right)
                nv.tensor_copy(shiftedf[:, 2, :], bif)
                step(nv.tensor_scalar(shifted[:, 1, :], bif, 2, None, ALU.logical_shift_right))
                step(nv.tensor_copy(shiftedf[:, 0:2, :], shifted))
                step(nv.scalar_tensor_tensor(bijf[:, 0, :], shiftedf[:, 1, :], -12.0, shiftedf[:, 0, :], ALU.add, ALU.max))
                nv.scalar_tensor_tensor(edge[:, 0, :], bijf[:, 0, :], -16.0, shiftedf[:, 2, :], ALU.mult, ALU.add)
                step(nv.scalar_tensor_tensor(edge[:, 1, :], bijf[:, 0, :], -4.0, shiftedf[:, 2, :], ALU.mult, ALU.add))
                step(nv.scalar_tensor_tensor(bijf[:, 1, :], edge[:, 1, :], -48.0, edge[:, 0, :], ALU.add, ALU.max))
                for c in range(2):
                    nv.tensor_tensor(pick[:, c, :, :], bijf[:, c, :].unsqueeze(2).to_broadcast([P, TT * TOPK, TOPK]),
                                     cst[:, K_IOTA:K_IOTA + TOPK].unsqueeze(1).to_broadcast([P, TT * TOPK, TOPK]),
                                     ALU.is_equal).then_inc(picks, 1)

            rank(0)
            with ve.Fori(1, HEADS) as i:
                step.enter(i - 1, 14)
                rank(i, finish_before=True)
                step.leave(HEADS - 1)
            finish(HEADS - 1)

            ve.wait_ge(slotsT_ready, 3)

            def u_low(r, e):
                ve.wait_ge(u_hi, r * RING + (e + 1))
                nv.tensor_tensor(us[:, e % 2, 1, :], ut[:, e, :], us[:, e % 2, 0, :].bitcast(F32), ALU.subtract).then_inc(u_split, 1)

            u_low(0, 0)
            u_low(0, 1)
            with ve.Fori(0, WITH_G // RING) as r:
                for e in range(RING):
                    for b in range(2):
                        ve.wait_ge(hot_done[b], r * 4 + e + FREE)
                        for q in range(4):
                            def col(f):
                                return slotsT[:, f, bass.ds(r * 32 + (e * 8 + b * 4 + q), 1)]
                            nv.tensor_scalar(ohi[:, b, q, :], cst[:, K_IOTA:K_IOTA + P], col(0), None, ALU.is_equal).then_inc(hot_ready[b], 1)
                            nv.tensor_scalar(ohj[:, b, q, :], cst[:, K_IOTA:K_IOTA + P], col(1), col(2), ALU.is_equal,
                                             ALU.mult).then_inc(hot_ready[b], 1)
                    u_low(r + (e + 2) // RING, (e + 2) % RING)
            with ve.Fori(WITH_G // RING, last_turn) as r:
                for e in range(RING):
                    u_low(r + (e + 2) // RING, (e + 2) % RING)
            for e in range(2):
                u_low(last_turn, e + 2)

            def weigh(r, e):
                b = e % 2
                ve.wait_ge(g_in[e], r * 32 + 32)
                nv.tensor_tensor(wgt[:, b, :], gl[:, e, :], gt[:, e, :], ALU.mult).then_inc(w_ready, 1)
                ve.wait_ge(v_hi, r * RING + (e + 1))
                nv.tensor_tensor(vs[:, b, 1, :], vt[:, e, :], vs[:, b, 0, :].bitcast(F32), ALU.subtract).then_inc(v_split, 1)
                ve.wait_ge(w_ready, r * RING + (e + 1))
                nv.tensor_copy(ar[:, b, 0, :], wgt[:, b, :]).then_inc(a_hi, 1)
                ve.wait_ge(a_hi, r * RING + (e + 1))
                nv.tensor_tensor(ar[:, b, 1, :], wgt[:, b, :], ar[:, b, 0, :].bitcast(F32), ALU.subtract).then_inc(a_split, 1)

            for e in range(RING):
                weigh(0, e)
            with ve.Fori(1, NK // RING) as r:
                for e in range(RING):
                    weigh(r, e)
            for k in range(DC):
                ve.wait_ge(bank_final, k + 1)
                nv.scalar_tensor_tensor(x[:, k, :], ps[k][:], part(5, k), x[:, k, :], ALU.mult, ALU.add).then_inc(x_ready, 1)
            inv_rms(3)
            ve.wait_ge(x_ready, 2 * DC)
            for k in range(DC):
                nv.scalar_tensor_tensor(h[:, k, :], x[:, k, :], sml[:, S_GF + k:S_GF + k + 1], rstd[:], ALU.mult, ALU.mult).then_inc(y_ready, 1)


def constants():
    k = np.zeros((P, K_END), np.float32)
    p, f = np.arange(P)[:, None], np.arange(P)[None, :]
    k[:, K_ID:K_ID + P] = p == f
    k[:, K_ONE:K_ONE + P] = 1.0
    k[:, K_NTRI:K_NTRI + P] = np.where(p >= f, -1.0, 0.0)
    k[:, K_NONE:K_NONE + P] = -1.0
    k[:, K_SBM:K_SBM + P] = np.where(p >= f, BIG, 0.0)
    k[:, K_CAUS:K_CAUS + P] = p < f
    half = HD // 2
    for m in range(P):
        if m % HD < half:
            k[m + half, K_ROT + m] = -1.0
        else:
            k[m - half, K_ROT + m] = 1.0
    k[:, K_IOTA:K_IOTA + P] = f
    q, c = np.arange(P)[:, None] // HD, np.arange(2 * P)[None, :] // HD - 2
    ok = (c == q) | (c == q - 1)
    k[:, K_SWA:K_SWA + 256] = np.where(ok, 0.0, BIG)
    k[:, K_NEVER:K_NEVER + P] = BIG
    k[:, K_INV] = np.float32(10000.0) ** (-(np.arange(P) % half).astype(np.float32) / np.float32(half))
    k[:, K_EPS] = EPS
    return k


def kernel(x, c, positions, norm1_g, norm2_g, final_g, w_ada, b_ada, w_in, sinks,
           w_up_swa, w_up_sb, w_out, w_query, sub_keys, expert_u, expert_v):
    import concourse.bacc as bacc
    from concourse.bass_utils import run_bass_kernel_spmd

    def columns(v):
        return np.asarray(v).reshape(-1, P).T

    def tiles(w):
        w = np.asarray(w)
        return w.reshape(w.shape[0] // P, P, w.shape[1]).transpose(1, 0, 2)

    order = np.array([h * HD + d for i in range(PAIRS) for h in (i, i + PAIRS) for d in range(HD)])
    pair_sinks = np.asarray(sinks)[0][[h for i in range(PAIRS) for h in (i, i + PAIRS)]]
    small = np.concatenate([columns(c[0]), columns(norm1_g[0]), columns(norm2_g[0]), columns(final_g),
                            columns(b_ada[0]), np.repeat(pair_sinks[None], P, 0)], 1)
    wi = np.asarray(w_in)[0]
    qa, kv, qb, kb, vb, g = (wi[:, 0:512][:, order], wi[:, 512:768], wi[:, 768:1280], wi[:, 1280:1792],
                             wi[:, 1792:2304], wi[:, 2304:])
    pair = np.stack([tiles(np.concatenate([w[:, i * P:(i + 1) * P] for w in (qa, qb, kb, vb)], 1)).reshape(P, -1)
                     for i in range(PAIRS)])
    gate = np.stack([tiles(np.concatenate([g[:, m * P:(m + 1) * P], g[:, D + m * P:D + (m + 1) * P]], 1)).reshape(P, -1)
                     for m in range(PAIRS)])
    ups = np.concatenate([np.asarray(w_up_swa)[0][order], np.asarray(w_up_sb)[0]], 0)
    sources = {"gate": g, "up": ups, "out": np.asarray(w_out)[0]}
    units = np.stack([tiles(sources[kind][:, c * D + m * P:c * D + (m + 1) * P]).reshape(P, -1) for kind, m, c in UNITS])
    wq = np.asarray(w_query)[0]
    qry = np.stack([tiles(wq[:, m * 256:(m + 1) * 256]).reshape(P, -1) for m in range(HEADS)])
    wa = np.asarray(w_ada)[0]
    ada = np.stack([tiles(wa[:, m * 512:(m + 1) * 512]).reshape(P, -1) for m in range(12)])
    skT = np.asarray(sub_keys)[0].reshape(2 * HEADS, NK, P).transpose(2, 0, 1)
    eu = np.asarray(expert_u)[0].reshape(NK, P, DC, P).transpose(0, 3, 2, 1).reshape(NK, P, DC * P)
    arrays = {
        "xT": tiles(np.asarray(x)[0].T), "small": small, "consts": constants(), "pos": np.asarray(positions),
        "w_ada": ada, "w_kava": tiles(kv), "w_pair": pair, "w_gate": gate, "w_units": units, "w_qry": qry,
        "skT": skT, "euT": eu, "ev": np.asarray(expert_v)[0].reshape(NK, P, D),
    }
    nc = bacc.Bacc("TRN2", target_bir_lowering=False, num_devices=1)
    arrays = {k: np.ascontiguousarray(a) for k, a in arrays.items()}
    args = [nc.dram_tensor(k, a.shape, mybir.dt.from_np(a.dtype), kind="ExternalInput").ap() for k, a in arrays.items()]
    args.append(nc.dram_tensor("outT", (P, DC, T), F32, kind="ExternalOutput").ap())
    build(nc, *args)
    got = run_bass_kernel_spmd(nc, [arrays], core_ids=[0]).results[0]["outT"]
    return np.ascontiguousarray(got.transpose(2, 1, 0)).reshape(1, T, D)
```
